# Optimizing a Trainium2 kernel written in Bass

```python
import jax
import jax.numpy as jnp
from jax import lax
import numpy as np

D_MODEL = 2048
BATCH = 1
SEQ = 256
DEPTH = 1

CHUNK = 64
MEM_LEN = 256
Q_BLOCK = 128
TOKEN_BLOCK = 128
EPS = 1e-6
ROPE_THETA = 10000.0

A_WIDTH = D_MODEL // 2
A_HEADS = 8
A_HEAD_DIM = A_WIDTH // A_HEADS
IDX_HEADS = 16
IDX_DIM = 64
TOP_K_MAX = 256

POOL_WIDTH = D_MODEL // 4
POOL_WINDOWS = (2, 4, 8, 16)
POOL_GROUP = POOL_WIDTH // 4

M_WIDTH = D_MODEL // 4
M_HEADS = 4
M_HEAD_DIM = M_WIDTH // M_HEADS

IN_SPLITS = (A_WIDTH, A_WIDTH, A_WIDTH, IDX_HEADS * IDX_DIM, IDX_DIM, IDX_HEADS, POOL_WIDTH, M_WIDTH)
IN_WIDTH = 3 * A_WIDTH + IDX_HEADS * IDX_DIM + IDX_DIM + IDX_HEADS + POOL_WIDTH + M_WIDTH
MIX_WIDTH = A_WIDTH + POOL_WIDTH + M_WIDTH

PEER_HEADS = 8
N_KEYS = 128
N_EXPERTS = N_KEYS * N_KEYS
PEER_TOPK = 16
PEER_KEY_DIM = 256

kernel_name = 'hybrid_dsa_pool_mem_peer_block'

def rms_norm(x, g):
    xf = x.astype(jnp.float32)
    y = xf * lax.rsqrt(jnp.mean(xf * xf, axis=-1, keepdims=True) + EPS)
    return (y * g.astype(jnp.float32)).astype(x.dtype)

def apply_rope(x, pos):
    half = x.shape[-1] // 2
    inv_freq = ROPE_THETA ** (-jnp.arange(half, dtype=jnp.float32) / half)
    ang = pos.astype(jnp.float32)[:, None] * inv_freq[None, :]
    cos = jnp.cos(ang)[None, :, None, :]
    sin = jnp.sin(ang)[None, :, None, :]
    xf = x.astype(jnp.float32)
    x1, x2 = xf[..., :half], xf[..., half:]
    return jnp.concatenate([x1 * cos - x2 * sin, x2 * cos + x1 * sin], axis=-1).astype(x.dtype)

def split_columns(z, widths):
    outs = []
    start = 0
    for w in widths:
        outs.append(z[..., start:start + w])
        start += w
    return outs

def dsa_sparse_attention(q, k, v, q_idx, k_idx, w_idx, pos):
    b, s, h, dh = q.shape
    top_k = min(TOP_K_MAX, s // 4)
    n_blk = s // Q_BLOCK
    key_chunk = pos // CHUNK
    scale = dh ** -0.5
    idx_scale = IDX_DIM ** -0.5

    def to_blocks(t):
        return jnp.swapaxes(t.reshape((b, n_blk, Q_BLOCK) + t.shape[2:]), 0, 1)

    def block(args):
        qb, qib, wb, qpos = args
        q_chunk = qpos // CHUNK
        raw = jnp.einsum('bqhd,bsd->bqhs', qib, k_idx) * idx_scale
        score = jnp.einsum('bqhs,bqh->bqs', jax.nn.relu(raw), wb).astype(jnp.float32)
        admissible = key_chunk[None, :] <= q_chunk[:, None]
        score = jnp.where(admissible[None], score, -jnp.inf)
        _, sel = lax.top_k(score, top_k)
        kg = jax.vmap(lambda kk, ii: kk[ii])(k, sel)
        vg = jax.vmap(lambda vv, ii: vv[ii])(v, sel)
        valid = (sel // CHUNK) <= q_chunk[None, :, None]
        logits = jnp.einsum('bqhd,bqkhd->bhqk', qb, kg).astype(jnp.float32) * scale
        logits = jnp.where(valid[:, None], logits, -jnp.inf)
        p = jax.nn.softmax(logits, axis=-1).astype(vg.dtype)
        return jnp.einsum('bhqk,bqkhd->bqhd', p, vg)

    out = lax.map(block, (to_blocks(q), to_blocks(q_idx), to_blocks(w_idx),
                          pos.reshape(n_blk, Q_BLOCK)))
    return jnp.swapaxes(out, 0, 1).reshape(b, s, h * dh)

def multiscale_pool_mixer(u, pool_w, pool_scale):
    b, s, c = u.shape
    uf = u.astype(jnp.float32)
    cs = jnp.concatenate([jnp.zeros((b, 1, c), jnp.float32), jnp.cumsum(uf, axis=1)], axis=1)
    t1 = jnp.arange(1, s + 1)
    outs = []
    for g, w in enumerate(POOL_WINDOWS):
        lo_c, hi_c = g * POOL_GROUP, (g + 1) * POOL_GROUP
        lo = jnp.maximum(t1 - w, 0)
        cnt = (t1 - lo).astype(jnp.float32)[None, :, None]
        csg = cs[:, :, lo_c:hi_c]
        mean = (csg[:, 1:] - csg[:, lo]) / cnt
        d = (mean - uf[:, :, lo_c:hi_c]).astype(u.dtype)
        outs.append(jnp.einsum('bsc,ce->bse', d, pool_w[g]))
    return jnp.concatenate(outs, axis=-1) * pool_scale

def memory_cross_attention(qm, km, vm):
    logits = jnp.einsum('bshd,bmhd->bhsm', qm, km).astype(jnp.float32) * (qm.shape[-1] ** -0.5)
    p = jax.nn.softmax(logits, axis=-1).astype(vm.dtype)
    out = jnp.einsum('bhsm,bmhd->bshd', p, vm)
    return out.reshape(qm.shape[0], qm.shape[1], -1)

def peer_ffn(x, w_q, sub_keys_1, sub_keys_2, u_tab, v_tab):
    b, s, d = x.shape
    n_tok = b * s
    t = x.reshape(n_tok, d)
    q = (t @ w_q).reshape(n_tok, PEER_HEADS, PEER_KEY_DIM)
    half = PEER_KEY_DIM // 2
    s1 = jnp.einsum('thd,nd->thn', q[..., :half], sub_keys_1).astype(jnp.float32)
    s2 = jnp.einsum('thd,nd->thn', q[..., half:], sub_keys_2).astype(jnp.float32)
    v1, i1 = lax.top_k(s1, PEER_TOPK)
    v2, i2 = lax.top_k(s2, PEER_TOPK)
    cand = (v1[..., :, None] + v2[..., None, :]).reshape(n_tok, PEER_HEADS, PEER_TOPK * PEER_TOPK)
    sc, ci = lax.top_k(cand, PEER_TOPK)
    e = (jnp.take_along_axis(i1, ci // PEER_TOPK, axis=-1) * N_KEYS
         + jnp.take_along_axis(i2, ci % PEER_TOPK, axis=-1))
    g = jax.nn.softmax(sc, axis=-1).astype(x.dtype)
    n_blk = n_tok // TOKEN_BLOCK

    def block(args):
        tb, eb, gb = args
        h = jnp.einsum('td,ted->te', tb, u_tab[eb])
        a = gb * jax.nn.gelu(h, approximate=False)
        return jnp.einsum('te,ted->td', a, v_tab[eb])

    out = lax.map(block, (t.reshape(n_blk, TOKEN_BLOCK, d),
                          e.reshape(n_blk, TOKEN_BLOCK, PEER_HEADS * PEER_TOPK),
                          g.reshape(n_blk, TOKEN_BLOCK, PEER_HEADS * PEER_TOPK)))
    return out.reshape(b, s, d)

def setup_inputs(seed: int = 0) -> dict:
    key = jax.random.key(seed)
    ks = jax.random.split(key, 20)
    f32 = jnp.float32

    def nrm(k, shape, scale):
        return jax.random.normal(k, shape, f32) * scale

    def gain(k, shape):
        return 1.0 + 0.02 * jax.random.normal(k, shape, f32)

    L = DEPTH
    return {
        'x': jax.random.normal(ks[0], (BATCH, SEQ, D_MODEL), f32),
        'mem': jax.random.normal(ks[1], (BATCH, MEM_LEN, D_MODEL), f32),
        'attn_norm_gain': gain(ks[2], (L, D_MODEL)),
        'w_in': nrm(ks[3], (L, D_MODEL, IN_WIDTH), D_MODEL ** -0.5),
        'q_norm_gain': gain(ks[4], (L, A_HEAD_DIM)),
        'k_norm_gain': gain(ks[5], (L, A_HEAD_DIM)),
        'pool_w': nrm(ks[6], (L, len(POOL_WINDOWS), POOL_GROUP, POOL_GROUP), POOL_GROUP ** -0.5),
        'pool_scale': gain(ks[7], (L, POOL_WIDTH)),
        'mem_norm_gain': gain(ks[8], (L, D_MODEL)),
        'w_mem_kv': nrm(ks[9], (L, D_MODEL, 2 * M_WIDTH), D_MODEL ** -0.5),
        'mq_norm_gain': gain(ks[10], (L, M_HEAD_DIM)),
        'mk_norm_gain': gain(ks[11], (L, M_HEAD_DIM)),
        'w_out': nrm(ks[12], (L, MIX_WIDTH, D_MODEL), MIX_WIDTH ** -0.5),
        'ffn_norm_gain': gain(ks[13], (L, D_MODEL)),
        'peer_w_q': nrm(ks[14], (L, D_MODEL, PEER_HEADS * PEER_KEY_DIM), D_MODEL ** -0.5),
        'peer_sub_keys_1': nrm(ks[15], (L, N_KEYS, PEER_KEY_DIM // 2), (PEER_KEY_DIM // 2) ** -0.5),
        'peer_sub_keys_2': nrm(ks[16], (L, N_KEYS, PEER_KEY_DIM // 2), (PEER_KEY_DIM // 2) ** -0.5),
        'peer_u': nrm(ks[17], (L, N_EXPERTS, D_MODEL), D_MODEL ** -0.5),
        'peer_v': nrm(ks[18], (L, N_EXPERTS, D_MODEL), 0.5),
    }

def reference(x, mem, attn_norm_gain, w_in, q_norm_gain, k_norm_gain, pool_w, pool_scale,
              mem_norm_gain, w_mem_kv, mq_norm_gain, mk_norm_gain, w_out,
              ffn_norm_gain, peer_w_q, peer_sub_keys_1, peer_sub_keys_2, peer_u, peer_v):
    b, s, _ = x.shape
    m = mem.shape[1]
    pos = jnp.arange(s)
    for l in range(DEPTH):
        xn = rms_norm(x, attn_norm_gain[l])
        z = jnp.einsum('bsd,de->bse', xn, w_in[l])
        q, k, v, qi, ki, wi, pu, qm = split_columns(z, IN_SPLITS)

        q = apply_rope(rms_norm(q.reshape(b, s, A_HEADS, A_HEAD_DIM), q_norm_gain[l]), pos)
        k = apply_rope(rms_norm(k.reshape(b, s, A_HEADS, A_HEAD_DIM), k_norm_gain[l]), pos)
        v = v.reshape(b, s, A_HEADS, A_HEAD_DIM)
        qi = apply_rope(qi.reshape(b, s, IDX_HEADS, IDX_DIM), pos)
        ki = apply_rope(ki[:, :, None, :], pos)[:, :, 0, :]
        wi = wi * (IDX_HEADS ** -0.5)
        a_out = dsa_sparse_attention(q, k, v, qi, ki, wi, pos)

        p_out = multiscale_pool_mixer(pu, pool_w[l], pool_scale[l])

        mn = rms_norm(mem, mem_norm_gain[l])
        kvm = jnp.einsum('bmd,de->bme', mn, w_mem_kv[l])
        km, vm = split_columns(kvm, (M_WIDTH, M_WIDTH))
        qm = rms_norm(qm.reshape(b, s, M_HEADS, M_HEAD_DIM), mq_norm_gain[l])
        km = rms_norm(km.reshape(b, m, M_HEADS, M_HEAD_DIM), mk_norm_gain[l])
        vm = vm.reshape(b, m, M_HEADS, M_HEAD_DIM)
        m_out = memory_cross_attention(qm, km, vm)

        mixed = jnp.concatenate([a_out, p_out, m_out], axis=-1)
        x = x + jnp.einsum('bse,ed->bsd', mixed, w_out[l])

        hn = rms_norm(x, ffn_norm_gain[l])
        x = x + peer_ffn(hn, peer_w_q[l], peer_sub_keys_1[l], peer_sub_keys_2[l], peer_u[l], peer_v[l])
    return x


_drawn_inputs = setup_inputs


def setup_inputs(seed=0):
    import zlib

    import numpy as np

    out = dict(_drawn_inputs(seed))
    spreads = {}
    factors = {'q_norm_gain': 14.053,
     'k_norm_gain': 11.666,
     'mem_norm_gain': 6.411,
     'mq_norm_gain': 6.713,
     'mk_norm_gain': 7.367,
     'pool_scale': 8.0,
     'ffn_norm_gain': 5.012}
    for name, (base, spread) in spreads.items():
        noise = np.random.default_rng([zlib.crc32(name.encode()), seed]).standard_normal(out[name].shape)
        drawn = base * np.exp(spread * noise) if base else spread * noise
        out[name] = jnp.asarray(drawn.astype(out[name].dtype))
    for name, factor in factors.items():
        out[name] = (out[name] * factor).astype(out[name].dtype)
    return out
```

```python
from contextlib import ExitStack

import concourse.bass as bass
from concourse import mybir
import numpy as np

F32 = mybir.dt.float32
F32R = mybir.dt.float32r
U32 = mybir.dt.uint32
ALU = mybir.AluOpType
ACT = mybir.ActivationFunctionType
AX_X = mybir.AxisListType.X

P = 128
D = 2048
S = 256
TB = S // P
KT = D // P
EPS = 1e-6
A_HEADS, M_HEADS, IDX_HEADS = 8, 4, 16
HEADS = A_HEADS + M_HEADS
TOP_K = 64
UNIT = 2048
C = 512
Z_CHUNKS = [("qi", 3072, C), ("qi", 3584, C), ("ki", 4096, 80), ("q", 0, C), ("q", 512, C), ("k", 1024, C),
            ("k", 1536, C), ("qm", 4688, C), ("pu", 4176, C), ("v", 2048, C), ("v", 2560, C)]
M_CHUNKS = [("km", 0, C), ("vm", 512, C)]
CHUNKS = Z_CHUNKS + M_CHUNKS
NZ = len(Z_CHUNKS)
UNITS_OF = [4 if w == C else 1 for _, _, w in CHUNKS]
FIRST_OF = [sum(UNITS_OF[:c]) for c in range(len(CHUNKS) + 1)]
N_MEM = FIRST_OF[NZ]
N_OUT = FIRST_OF[-1]
N_WQ = N_OUT + 16
N_EXP = N_WQ + 16
HALF = 64
N_ALL = N_EXP + 4 * HALF
TR_CHUNKS = [c for c, (name, _, _) in enumerate(CHUNKS) if name in ("qi", "ki", "q", "k", "qm", "km")]
IDX_AT = {4: 0, 5: 2, 6: 4, 7: 6}
PEER_HEADS, PEER_K = 8, 16
SLOTS = PEER_HEADS * PEER_K
GT = 8
GROUPS = S // GT
LP = 1152
NOT_ADMISSIBLE = -1e38
TAKEN = -3e38
ATT_SCALE = 128.0 ** -0.5
IDX_SCALE = 64.0 ** -0.5


def u_first(half):
    return N_EXP + 2 * HALF * half


def v_first(half):
    return u_first(half) + HALF


def build(nc, a, out):
    with ExitStack() as ctx:
        def sb(name, shape, dt=F32):
            return ctx.enter_context(nc.sbuf_tensor(name, shape, dt))

        def sem(name):
            return ctx.enter_context(nc.semaphore(name))

        resid = sb("resid", [P, TB, D])
        big = sb("big", [P, HALF * S])
        XT = sb("XT", [P, KT, 2, S], F32R)
        raw = sb("raw", [P, 2, UNIT])
        hi = sb("hi", [P, 2, UNIT], F32R)
        lo = sb("lo", [P, 2, UNIT], F32R)
        ah = sb("ah", [P, 2, S], F32R)
        al = sb("al", [P, 2, S], F32R)
        scr = sb("scr", [P, 8448])
        cst = sb("cst", [P, 576])
        ident, iota = cst[:, 0:128], cst[:, 128:256]
        keysT = cst[:, 256:512].rearrange("p (s n) -> p s n", s=2)
        gains = cst[:, 512:512 + 3 * KT].rearrange("p (r k) -> p r k", r=3)
        pscale = cst[:, 560:564]
        ssq = cst[:, 570:572]
        var = cst[:, 564:566]
        rstd = cst[:, 566:568]

        acts = big[:, :].rearrange("p (j t) -> p j t", j=HALF)
        xs = big[:, 0:4096].rearrange("p (b d) -> p b d", b=TB)
        v_sb = big[:, 0:2048].rearrange("p (b d) -> p b d", b=TB)
        pu_sb = big[:, 2048:3072].rearrange("p (b d) -> p b d", b=TB)
        vm_sb = big[:, 3072:4096].rearrange("p (b d) -> p b d", b=TB)
        ms = big[:, 4096:8192].rearrange("p (b d) -> p b d", b=TB)
        prob = big[:, 4096:5120].rearrange("p (r b s) -> p r b s", r=2, b=TB)
        probT = big[:, 5120:6144].rearrange("p (r b s) -> p r b s", r=2, b=TB)
        poolM = big[:, 6144:8192].rearrange("p (g b t) -> p g b t", g=4, b=TB)
        qT = big[:, 8192:10240].rearrange("p (h t) -> p h t", h=8)
        kT = big[:, 10240:12288].rearrange("p (h t) -> p h t", h=8)
        qiT = big[:, 12288:14336].rearrange("p (h t) -> p h t", h=8)
        qmT = big[:, 14336:15360].rearrange("p (h t) -> p h t", h=4)
        kmT = big[:, 15360:16384].rearrange("p (h t) -> p h t", h=4)
        hs = big[:, 8192:12288].rearrange("p (b d) -> p b d", b=TB)

        zt = scr[:, 0:2048].rearrange("p (r b d) -> p r b d", r=2, b=TB)
        tmpA = scr[:, 2048:3072]
        tmpB = scr[:, 3072:4096]
        score = scr[:, 4096:4608].rearrange("p (b s) -> p b s", b=TB)
        mbias = scr[:, 4608:5120].rearrange("p (b s) -> p b s", b=TB)
        relu = scr[:, 5120:6144].rearrange("p (h j s) -> p h j s", h=2, j=2)
        pooldT = scr[:, 5120:6144].rearrange("p (g t) -> p g t", g=4)
        kiT = scr[:, 6144:6400]
        kidup = scr[:, 6400:6656].rearrange("p (b d) -> p b d", b=TB)
        wi = scr[:, 6656:6688].rearrange("p (b h) -> p b h", b=TB)
        top8 = scr[:, 6688:6696]
        hstat = scr[:, 6696:6720].rearrange("p (n h) -> p n h", n=3)
        astat = scr[:, 6720:6736].rearrange("p (r n b) -> p r n b", r=2, n=4)
        hgain = scr[:, 6784:7296].rearrange("p (n d) -> p n d", n=4)
        ropeA = scr[:, 7296:7552].rearrange("p (n b f) -> p n b f", n=2, b=TB)
        ropeI = scr[:, 7552:7680].rearrange("p (n b f) -> p n b f", n=2, b=TB)
        poolW = scr[:, 7680:8192].rearrange("p (g e) -> p g e", g=4)

        sc_all = scr[:, 0:4096].rearrange("p (b m n) -> p b m n", b=TB, m=16)
        selA = scr[:, 0:2048].rearrange("p (h k a) -> p h k a", h=8, k=16)
        oh1 = scr[:, 0:2048].rearrange("p (r t n) -> p r t n", r=2, t=GT)
        oh2 = scr[:, 2048:3072].rearrange("p (r t n) -> p r t n", r=2, t=GT)
        v16 = scr[:, 4096:4608].rearrange("p (b m a) -> p b m a", b=TB, m=16)
        ix16 = scr[:, 4608:5120].bitcast(U32).rearrange("p (b m a) -> p b m a", b=TB, m=16)
        ixf = scr[:, 5120:5632].rearrange("p (b m a) -> p b m a", b=TB, m=16)
        cand = scr[:, 5632:5888]
        pick = scr[:, 5888:6144].rearrange("p (b h k) -> p b h k", b=TB, h=8)
        ci = scr[:, 6144:6400].bitcast(U32).rearrange("p (b s) -> p b s", b=TB)
        cab = scr[:, 6400:6912].bitcast(U32).rearrange("p (n b s) -> p n b s", n=2, b=TB)
        abf = scr[:, 6912:7424].rearrange("p (n b s) -> p n b s", n=2, b=TB)
        slotT = scr[:, 7424:8192].rearrange("p (n t) -> p n t", n=3)
        qTr = scr[:, 7424:7936].rearrange("p (r t) -> p r t", r=2)
        gsum = scr[:, 8192:8208].rearrange("p (b h) -> p b h", b=TB)
        isel = scr[:, 6912:7424].rearrange("p (n b s) -> p n b s", n=2, b=TB)

        bank = [ctx.enter_context(nc.psum_tensor(f"bank{i}", [P, 512], F32)) for i in range(8)]

        const_in = sem("const_in")
        x_in = sem("x_in")
        mem_in = sem("mem_in")
        poolm_in = sem("poolm_in")
        raw_in = [sem("raw_in0"), sem("raw_in1")]
        hi_done = sem("hi_done")
        lo_dve_done = sem("lo_dve_done")
        lo_pool_done = sem("lo_pool_done")
        pe_used = sem("pe_used")
        ssq_done = sem("ssq_done")
        var_done = sem("var_done")
        std_done = sem("std_done")
        rows_scaled = sem("rows_scaled")
        xt_psum = sem("xt_psum")
        xt_hi = sem("xt_hi")
        xt_lo = sem("xt_lo")
        z_evac = sem("z_evac")
        z_ready = sem("z_ready")
        hvar_done = sem("hvar_done")
        hstd_done = sem("hstd_done")
        tr_psum = sem("tr_psum")
        tr_evac = sem("tr_evac")
        idx_psum = sem("idx_psum")
        idx_relu = sem("idx_relu")
        idx_added = sem("idx_added")
        poold_psum = sem("poold_psum")
        poold_evac = sem("poold_evac")
        poolw_psum = sem("poolw_psum")
        logit_psum = sem("logit_psum")
        logit_masked = sem("logit_masked")
        prob_exp = sem("prob_exp")
        prob_ready = sem("prob_ready")
        probT_psum = sem("probT_psum")
        probT_evac = sem("probT_evac")
        av_psum = sem("av_psum")
        h_added = sem("h_added")
        wq_evac = sem("wq_evac")
        key_psum = sem("key_psum")
        key_evac = sem("key_evac")
        gelu_done = sem("gelu_done")
        pick_shift = sem("pick_shift")
        pick_exp = sem("pick_exp")
        slots_ready = sem("slots_ready")
        slots_psum = sem("slots_psum")
        slots_evac = sem("slots_evac")
        oh1_done = sem("oh1_done")
        oh2_done = sem("oh2_done")
        oh2_eq = sem("oh2_eq")
        g_psum = sem("g_psum")
        g_applied = sem("g_applied")
        ah_done = sem("ah_done")
        al_done = sem("al_done")
        v_added = sem("v_added")
        out_done = sem("out_done")
        dve_step = sem("dve_step")

        N_CONST = 3
        block = ctx.enter_context(nc.Block())

        def lo_waits(eng, n, slot):
            eng.wait_ge(hi_done, n + 1)
            if isinstance(n, int) and n < 2:
                return
            eng.wait_ge(pe_used, n - 1)

        @block.sync
        def _(sp):
            def load_unit(n, slot, src):
                if not (isinstance(n, int) and n < 2):
                    sp.wait_ge(hi_done, n - 1)
                    sp.wait_ge(lo_dve_done, n - 1)
                    sp.wait_ge(lo_pool_done, n - 1)
                sp.dma_start(raw[:, slot, 0:src.shape[-1]], src).then_inc(raw_in[slot], 16)

            sp.dma_start(resid[:, :, :], a["x"].rearrange("(b p) d -> p b d", p=P)).then_inc(x_in, 16)
            sp.dma_start(cst[:, 0:564], a["c_main"]).then_inc(const_in, 16)
            sp.dma_start(scr[:, 6784:8192], a["c_mix"]).then_inc(const_in, 16)
            sp.dma_start(score, a["c_adm"]).then_inc(const_in, 16)
            n = 0
            for c, (name, _, w) in enumerate(CHUNKS):
                for u in range(UNITS_OF[c]):
                    if name == "ki":
                        src = a["w_ki"]
                    else:
                        src = a["w_mix"][n if n < 8 else n - 1]
                    load_unit(n, n % 2, src)
                    if n == 1:
                        sp.dma_start(ms[:, :, :], a["mem"].rearrange("(b p) d -> p b d", p=P)).then_inc(mem_in, 16)
                    n += 1
            for _ in range(32):
                load_unit(n, n % 2, a["w_mix"][n - 1])
                n += 1
            for half in range(2):
                n0 = u_first(half)
                with sp.Fori(0, HALF // 2) as i:
                    for s in range(2):
                        load_unit(i * 2 + (n0 + s), (n0 + s) % 2,
                                  a["u"][bass.ds(i * 2 + (half * HALF + s), 1), :, :].rearrange("o p f -> p (o f)"))
                n0 = v_first(half)
                with sp.Fori(0, HALF // 2) as i:
                    for s in range(2):
                        load_unit(i * 2 + (n0 + s), (n0 + s) % 2,
                                  a["v"][:, bass.ds(i * 2 + (half * HALF + s), 1), :].rearrange("p o f -> p (o f)"))
            for b in range(TB):
                sp.wait_ge(v_added, 8 + 4 * (b + 1))
                sp.dma_start(out[b * P:(b + 1) * P, :], resid[:, b, :]).then_inc(out_done, 16)
            sp.wait_ge(out_done, 16 * TB)

        @block.gpsimd
        def _(pool):
            def lo_pool(n, slot):
                lo_waits(pool, n, slot)
                nc.gpsimd.tensor_tensor(lo[:, slot, 0:LP], raw[:, slot, 0:LP], hi[:, slot, 0:LP].bitcast(F32),
                                        ALU.subtract).then_inc(lo_pool_done, 1)

            lo_pool(0, 0)
            lo_pool(1, 1)
            with pool.Fori(0, (N_MEM - 3) // 2) as i:
                for s in range(2):
                    lo_pool(i * 2 + (2 + s), s)
            lo_pool(N_MEM - 1, 0)
            lo_pool(N_MEM, 1)
            lo_pool(N_MEM + 1, 0)
            pool.wait_ge(xt_psum, 16)
            pool.dma_start(poolM, a["c_pool"]).then_inc(poolm_in, 16)
            with pool.Fori(0, (N_EXP + HALF - N_MEM) // 2) as i:
                for s in range(2):
                    lo_pool(i * 2 + (N_MEM + 2 + s), (N_MEM + s) % 2)

            for half in range(2):
                pool.wait_ge(slots_evac, 3)

                def weigh_one_hot(i, s):
                    g = i * 2 + (half * GROUPS + s)
                    t0 = i * (2 * GT) + s * GT
                    pool.wait_ge(oh2_eq, g + 1)
                    nc.gpsimd.tensor_tensor(
                        oh2[:, s, :, :], oh2[:, s, :, :],
                        slotT[:, 2, bass.ds(t0, GT)].unsqueeze(2).to_broadcast([P, GT, HALF]),
                        ALU.mult).then_inc(oh2_done, 1)

                with pool.Fori(0, GROUPS // 2) as i:
                    for s in range(2):
                        weigh_one_hot(i, s)
                count = 2 * HALF if half == 0 else HALF - 2
                n0 = v_first(half) + 2
                with pool.Fori(0, count // 2) as i:
                    for s in range(2):
                        lo_pool(i * 2 + (n0 + s), (n0 + s) % 2)

        @block.scalar
        def _(act):
            def make_hi(n, slot):
                if isinstance(n, int):
                    act.wait_ge(raw_in[slot], 16 * (n // 2 + 1))
                    if n >= 2:
                        act.wait_ge(pe_used, n - 1)
                nc.scalar.activation(hi[:, slot, :], raw[:, slot, :], ACT.Copy).then_inc(hi_done, 1)

            def make_hi_loop(i, n0):
                act.wait_ge(raw_in[n0 % 2], i * 16 + 16 * (n0 // 2 + 1))
                act.wait_ge(pe_used, i * 2 + (n0 - 1))
                nc.scalar.activation(hi[:, n0 % 2, :], raw[:, n0 % 2, :], ACT.Copy).then_inc(hi_done, 1)

            def row_squares(src, junk):
                for b in range(TB):
                    ins = nc.scalar.activation(junk[:, b, :], src[:, b, :], ACT.Square, accum_out=ssq[:, b:b + 1])
                ins.then_inc(ssq_done, 1)

            def row_std(r):
                act.wait_ge(var_done, r + 1)
                nc.scalar.activation(rstd, var, ACT.Sqrt).then_inc(std_done, 1)

            def xt_high(r):
                for k in range(KT):
                    act.wait_ge(xt_psum, 8 * r + k // 2 + 1)
                    src = bank[k // 2][:, (k % 2) * S:(k % 2 + 1) * S]
                    nc.scalar.activation(XT[:, k, 0, :], src, ACT.Copy, scale=gains[:, r, k:k + 1]).then_inc(xt_hi, 1)

            def evac_chunk(c):
                name, _, w = CHUNKS[c]
                act.wait_ge(pe_used, FIRST_OF[c + 1])
                dst = {"pu": pu_sb, "vm": vm_sb}.get(name, zt[:, c % 2])
                if name == "v":
                    dst = v_sb[:, :, (c - 9) * C:(c - 8) * C]
                elif name not in ("pu", "vm"):
                    earlier = [t for t in range(len(TR_CHUNKS)) if TR_CHUNKS[t] < c and TR_CHUNKS[t] % 2 == c % 2]
                    if earlier:
                        act.wait_ge(tr_psum, earlier[-1] + 1)
                for b in range(TB):
                    ins = nc.scalar.activation(dst[:, b, 0:w], bank[2 * (c % 2) + b][:, 0:w], ACT.Copy)
                ins.then_inc(z_evac, 1)

            def head_std(c):
                order = [x for x, (name, _, _) in enumerate(CHUNKS) if name in ("q", "k", "qm", "km")]
                if c in order:
                    act.wait_ge(hvar_done, order.index(c) + 1)
                    nc.scalar.activation(hstat[:, 2, :], hstat[:, 1, :], ACT.Sqrt).then_inc(hstd_done, 1)

            def evac_transposed(t):
                c = TR_CHUNKS[t]
                name, first, _ = CHUNKS[c]
                act.wait_ge(tr_psum, t + 1)
                if name == "ki":
                    nc.scalar.activation(kiT, bank[4][:, 0:S], ACT.Copy).then_inc(tr_evac, 1)
                    return
                dst = {"qi": qiT, "q": qT, "k": kT, "qm": qmT, "km": kmT}[name]
                at = 4 * (first // C % 2) if name in ("qi", "q", "k") else 0
                for g in range(2):
                    ins = nc.scalar.activation(dst[:, at + 2 * g:at + 2 * g + 2, :],
                                               bank[4 + g][:, :].rearrange("p (h t) -> p h t", h=2), ACT.Copy)
                ins.then_inc(tr_evac, 1)

            def index_relu(g):
                act.wait_ge(idx_psum, g + 1)
                if g >= 1:
                    act.wait_ge(idx_added, g)
                for h in range(2):
                    ins = nc.scalar.activation(relu[:, h, :, :], bank[6 + h][:, :].rearrange("p (j s) -> p j s", j=2),
                                               ACT.Relu, scale=IDX_SCALE)
                ins.then_inc(idx_relu, 1)

            act.wait_ge(x_in, 16)
            row_squares(resid, xs)
            row_std(0)
            act.wait_ge(mem_in, 16)
            act.wait_ge(rows_scaled, 1)
            row_squares(ms, hs)
            row_std(1)
            act.wait_ge(const_in, 16 * N_CONST)
            xt_high(0)
            for c in range(len(CHUNKS) + 1):
                if c < len(CHUNKS):
                    make_hi(FIRST_OF[c], FIRST_OF[c] % 2)
                if c >= 1:
                    evac_chunk(c - 1)
                if c - 1 in IDX_AT:
                    for g in range(IDX_AT[c - 1], IDX_AT[c - 1] + 2):
                        index_relu(g)
                if c == NZ:
                    xt_high(1)
                if c >= 1 and c < len(CHUNKS) and UNITS_OF[c] > 1:
                    make_hi(FIRST_OF[c] + 1, (FIRST_OF[c] + 1) % 2)
                if c >= 1:
                    head_std(c - 1)
                if c == 0:
                    make_hi(1, 1)
                if c - 2 in TR_CHUNKS:
                    evac_transposed(TR_CHUNKS.index(c - 2))
                if c < len(CHUNKS):
                    for u in range(2, UNITS_OF[c]):
                        make_hi(FIRST_OF[c] + u, (FIRST_OF[c] + u) % 2)
            make_hi(N_OUT, N_OUT % 2)
            make_hi(N_OUT + 1, (N_OUT + 1) % 2)
            for g in range(2):
                act.wait_ge(poold_psum, g + 1)
                nc.scalar.activation(pooldT[:, 2 * g:2 * g + 2, :], bank[6 + g][:, :].rearrange("p (g t) -> p g t", g=2),
                                     ACT.Copy).then_inc(poold_evac, 1)
            for i in range(HEADS + 2):
                if i < HEADS:
                    r = i % 2
                    act.wait_ge(logit_masked, i + 1)
                    for b in range(TB):
                        ins = nc.scalar.activation(prob[:, r, b, :], prob[:, r, b, :], ACT.Exp,
                                                   bias=astat[:, r, 0, b:b + 1], accum_out=astat[:, r, 1, b:b + 1])
                    ins.then_inc(prob_exp, 1)
                if 0 <= i - 1 < HEADS:
                    act.wait_ge(probT_psum, i)
                    if i - 1 >= 2:
                        act.wait_ge(av_psum, i - 2)
                    nc.scalar.activation(probT[:, (i - 1) % 2, :, :],
                                         bank[2 + (i - 1) % 2][:, :].rearrange("p (b s) -> p b s", b=TB),
                                         ACT.Copy).then_inc(probT_evac, 1)
                if i == 1:
                    for g in range(4):
                        act.wait_ge(poolw_psum, g // 2 + 1)
                        nc.scalar.activation(XT[:, 8 + g, 0, :], bank[6 + g // 2][:, (g % 2) * S:(g % 2 + 1) * S],
                                             ACT.Copy, scale=pscale[:, g:g + 1]).then_inc(xt_hi, 1)
                if i >= 2:
                    h = i - 2
                    act.wait_ge(av_psum, h + 1)
                    k = h if h < A_HEADS else h + 4
                    nc.scalar.activation(XT[:, k, 0, :], bank[4 + h % 2][:, 0:S], ACT.Copy).then_inc(xt_hi, 1)
            for n in range(N_OUT + 2, N_WQ + 2):
                make_hi(n, n % 2)
            act.wait_ge(h_added, 4)
            row_squares(resid, hs)
            row_std(2)
            xt_high(2)
            for m in range(16):
                n = N_WQ + m
                act.wait_ge(pe_used, n + 1)
                if m >= 2:
                    act.wait_ge(key_psum, m - 1)
                nc.scalar.activation(qTr[:, m % 2, :], bank[m % 2][:, 0:S], ACT.Copy).then_inc(wq_evac, 1)
                make_hi(n + 2, n % 2)
            for half in range(2):
                n0 = u_first(half)
                with act.Fori(0, HALF // 2) as i:
                    for s in range(2):
                        act.wait_ge(pe_used, i * 2 + (n0 + s + 1))
                        nc.scalar.activation(acts[:, bass.ds(i * 2 + s, 1), :], bank[(n0 + s) % 2][:, 0:S].unsqueeze(1),
                                             ACT.Gelu).then_inc(gelu_done, 1)
                        make_hi_loop(i, n0 + s + 2)
                if half == 0:
                    act.wait_ge(pick_shift, 1)
                    nc.scalar.activation(pick, pick, ACT.Exp).then_inc(pick_exp, 1)
                    for x in range(3):
                        act.wait_ge(slots_psum, x + 1)
                        nc.scalar.activation(slotT[:, x, :], bank[4 + x][:, 0:S], ACT.Copy).then_inc(slots_evac, 1)
                n0 = v_first(half)
                act.wait_ge(g_applied, GROUPS * (half + 1))
                for s in range(2):
                    nc.scalar.activation(ah[:, s, :], acts[:, s, :], ACT.Copy).then_inc(ah_done, 1)
                with act.Fori(0, HALF // 2 - 1) as i:
                    for s in range(2):
                        make_hi_loop(i, n0 + s + 2)
                        nc.scalar.activation(ah[:, s, :], acts[:, bass.ds(i * 2 + (s + 2), 1), :].rearrange("p o t -> p (o t)"),
                                             ACT.Copy).then_inc(ah_done, 1)
                if half == 0:
                    for s in range(2):
                        make_hi(n0 + HALF + s, (n0 + HALF + s) % 2)

        @block.vector
        def _(dve):
            steps = [0]

            def link(ins):
                steps[0] += 1
                ins.then_inc(dve_step, 1)
                dve.wait_ge(dve_step, steps[0])

            tt = nc.vector.tensor_tensor

            def lo_dve(n, slot):
                lo_waits(dve, n, slot)
                tt(lo[:, slot, LP:UNIT], raw[:, slot, LP:UNIT], hi[:, slot, LP:UNIT].bitcast(F32),
                   ALU.subtract).then_inc(lo_dve_done, 1)

            def row_scale(r, src, dst):
                dve.wait_ge(ssq_done, r + 1)
                nc.vector.tensor_scalar(var, ssq, 1.0 / D, EPS, ALU.mult, ALU.add).then_inc(var_done, 1)
                dve.wait_ge(std_done, r + 1)
                link(nc.vector.reciprocal(rstd, rstd))
                for b in range(TB):
                    ins = nc.vector.tensor_scalar(dst[:, b, :], src[:, b, :], rstd[:, b:b + 1], None, ALU.mult)
                ins.then_inc(rows_scaled, 1)

            def xt_low(r):
                for k in range(KT):
                    dve.wait_ge(xt_hi, (0, 16, 48)[r] + (k | 1) + 1)
                    src = bank[k // 2][:, (k % 2) * S:(k % 2 + 1) * S]
                    nc.vector.scalar_tensor_tensor(XT[:, k, 1, :], src, gains[:, r, k:k + 1],
                                                   XT[:, k, 0, :].bitcast(F32), ALU.mult, ALU.subtract).then_inc(xt_lo, 1)

            normed = [x for x, (name, _, _) in enumerate(CHUNKS) if name in ("q", "k", "qm", "km")]

            def heads_a(c):
                if c not in normed:
                    return
                z = zt[:, c % 2].rearrange("p b (h d) -> p (b h) d", d=P)
                t = tmpA.rearrange("p (h d) -> p h d", d=P)
                dve.wait_ge(z_evac, c + 1)
                link(tt(t, z, z, ALU.mult))
                link(nc.vector.tensor_reduce(hstat[:, 0, :], t, AX_X, ALU.add))
                nc.vector.tensor_scalar(hstat[:, 1, :], hstat[:, 0, :], 1.0 / P, EPS, ALU.mult, ALU.add)\
                    .then_inc(hvar_done, 1)

            def signal_ready(ins, c):
                ins.then_inc(z_ready, 1)
                dve.wait_ge(z_ready, TR_CHUNKS.index(c) + 1)

            def heads_b(c):
                name = CHUNKS[c][0]
                if name in ("pu", "v", "vm"):
                    return
                dve.wait_ge(z_evac, c + 1)
                z = zt[:, c % 2]
                if c in normed:
                    z3 = z.rearrange("p b (h d) -> p (b h) d", d=P)
                    dve.wait_ge(hstd_done, normed.index(c) + 1)
                    link(nc.vector.reciprocal(hstat[:, 2, :], hstat[:, 2, :]))
                    link(tt(z3, z3, hstat[:, 2, :].unsqueeze(2).to_broadcast([P, 8, P]), ALU.mult))
                    gain = hgain[:, ("q", "k", "qm", "km").index(name), :].unsqueeze(1).to_broadcast([P, 8, P])
                    ins = tt(z3, z3, gain, ALU.mult)
                    if name in ("qm", "km"):
                        signal_ready(ins, c)
                        return
                    link(ins)
                rope = ropeA if name in ("q", "k") else ropeI
                f = 64 if name in ("q", "k") else 32
                w = 64 if name == "ki" else C
                nh = w // f
                z4 = z[:, :, 0:w].rearrange("p b (h f) -> p b h f", f=f)
                tA = tmpA[:, 0:2 * w].rearrange("p (b h f) -> p b h f", b=TB, f=f)
                tB = tmpB[:, 0:2 * w].rearrange("p (b h f) -> p b h f", b=TB, f=f)
                tt(tA, z4, rope[:, 0, :, :].unsqueeze(2).to_broadcast([P, TB, nh, f]), ALU.mult)
                link(tt(tB, z4, rope[:, 1, :, :].unsqueeze(2).to_broadcast([P, TB, nh, f]), ALU.mult))
                a5 = tmpA[:, 0:2 * w].rearrange("p (b h g f) -> p b h g f", b=TB, g=2, f=f)
                b5 = tmpB[:, 0:2 * w].rearrange("p (b h g f) -> p b h g f", b=TB, g=2, f=f)
                if name != "ki":
                    z5 = z.rearrange("p b (h g f) -> p b h g f", g=2, f=f)
                    tt(z5[:, :, :, 0, :], a5[:, :, :, 0, :], b5[:, :, :, 1, :], ALU.subtract)
                    signal_ready(tt(z5[:, :, :, 1, :], a5[:, :, :, 1, :], b5[:, :, :, 0, :], ALU.add), c)
                    return
                for copy in range(2):
                    tt(kidup[:, :, 64 * copy:64 * copy + f], a5[:, :, 0, 0, :], b5[:, :, 0, 1, :], ALU.subtract)
                    tt(kidup[:, :, 64 * copy + f:64 * copy + 2 * f], a5[:, :, 0, 1, :], b5[:, :, 0, 0, :], ALU.add)
                signal_ready(nc.vector.tensor_scalar(wi, z[:, :, 64:80], IDX_HEADS ** -0.5, None, ALU.mult), c)

            def index_add(g):
                b = g // 4
                dve.wait_ge(idx_relu, g + 1)
                for j in range(2):
                    for h in range(2):
                        head = 2 * (2 * (g % 4) + j) + h
                        ins = nc.vector.scalar_tensor_tensor(score[:, b, :], relu[:, h, j, :], wi[:, b, head:head + 1],
                                                             score[:, b, :], ALU.mult, ALU.add)
                        if (j, h) != (1, 1):
                            link(ins)
                ins.then_inc(idx_added, 1)
                dve.wait_ge(idx_added, g + 1)

            def take_eight(b):
                link(nc.vector.max(top8, score[:, b, :]))
                link(nc.vector.match_replace(score[:, b, :], top8, score[:, b, :], TAKEN))

            dve.wait_ge(x_in, 16)
            row_scale(0, resid, xs)
            dve.wait_ge(mem_in, 16)
            row_scale(1, ms, ms)
            dve.wait_ge(const_in, 16 * N_CONST)
            xt_low(0)
            for c in range(len(CHUNKS) + 1):
                units = UNITS_OF[c] if c < len(CHUNKS) else 0
                n = FIRST_OF[c]
                if units:
                    lo_dve(n, n % 2)
                if c >= 1:
                    heads_a(c - 1)
                if c - 1 in IDX_AT:
                    for g in range(IDX_AT[c - 1], IDX_AT[c - 1] + 2):
                        index_add(g)
                if c == NZ:
                    xt_low(1)
                if units > 1:
                    lo_dve(n + 1, (n + 1) % 2)
                if c >= 1:
                    heads_b(c - 1)
                for u in range(2, units):
                    lo_dve(n + u, (n + u) % 2)
                    if c in (9, 10):
                        for _ in range(4):
                            take_eight(c - 9)
            for b in range(TB):
                link(nc.vector.tensor_scalar(mbias[:, b, :], score[:, b, :], 0.5 * (TAKEN + NOT_ADMISSIBLE), -1e30,
                                             ALU.is_gt, ALU.mult))
            lo_dve(N_OUT, N_OUT % 2)
            lo_dve(N_OUT + 1, (N_OUT + 1) % 2)
            for i in range(HEADS + 2):
                if i < HEADS:
                    r = i % 2
                    dve.wait_ge(logit_psum, i + 1)
                    if i >= 2:
                        dve.wait_ge(probT_psum, i - 1)
                    src = bank[r][:, :].rearrange("p (b s) -> p b s", b=TB)
                    if i < A_HEADS:
                        link(nc.vector.scalar_tensor_tensor(prob[:, r, :, :], src, ATT_SCALE, mbias, ALU.mult, ALU.add))
                    else:
                        link(nc.vector.tensor_scalar(prob[:, r, :, :], src, ATT_SCALE, None, ALU.mult))
                    link(nc.vector.tensor_reduce(astat[:, r, 2, :], prob[:, r, :, :], AX_X, ALU.max))
                    nc.vector.tensor_scalar(astat[:, r, 0, :], astat[:, r, 2, :], -1.0, None, ALU.mult)\
                        .then_inc(logit_masked, 1)
                    dve.wait_ge(prob_exp, i + 1)
                    link(nc.vector.reciprocal(astat[:, r, 3, :], astat[:, r, 1, :]))
                    for b in range(TB):
                        ins = nc.vector.tensor_scalar(prob[:, r, b, :], prob[:, r, b, :], astat[:, r, 3, b:b + 1],
                                                      None, ALU.mult)
                    ins.then_inc(prob_ready, 1)
                if i == 1:
                    for g in range(4):
                        dve.wait_ge(xt_hi, 32 + (g | 1) + 1)
                        nc.vector.scalar_tensor_tensor(XT[:, 8 + g, 1, :], bank[6 + g // 2][:, (g % 2) * S:(g % 2 + 1) * S],
                                                       pscale[:, g:g + 1], XT[:, 8 + g, 0, :].bitcast(F32),
                                                       ALU.mult, ALU.subtract).then_inc(xt_lo, 1)
                if i >= 2:
                    h = i - 2
                    k = h if h < A_HEADS else h + 4
                    dve.wait_ge(xt_hi, 36 + h + 1)
                    tt(XT[:, k, 1, :], bank[4 + h % 2][:, 0:S], XT[:, k, 0, :].bitcast(F32), ALU.subtract)\
                        .then_inc(xt_lo, 1)
            for oc in range(5):
                n = N_OUT + 4 * oc
                if oc >= 1:
                    dve.wait_ge(pe_used, n)
                    for b in range(TB):
                        r = resid[:, b, (oc - 1) * C:oc * C]
                        ins = tt(r, r, bank[2 * ((oc - 1) % 2) + b][:, :], ALU.add)
                    ins.then_inc(h_added, 1)
                if oc < 4:
                    for u in range(2, 6):
                        lo_dve(n + u, (n + u) % 2)
            row_scale(2, resid, hs)
            xt_low(2)
            for m in range(17):
                n = N_WQ + m
                if m < 16:
                    lo_dve(n + 2, n % 2)
                if m >= 1:
                    dve.wait_ge(key_psum, m)
                    nc.vector.tensor_copy(sc_all[:, :, m - 1, :],
                                          bank[4 + (m - 1) % 2][:, 0:S].rearrange("p (b n) -> p b n", b=TB))\
                        .then_inc(key_evac, 1)
            dve.wait_ge(key_evac, 16)

            def top16(values, best, where):
                link(nc.vector.max(best[:, 0:8], values))
                link(nc.vector.max_index(where[:, 0:8], best[:, 0:8], values))
                link(nc.vector.match_replace(values, best[:, 0:8], values, TAKEN))
                link(nc.vector.max(best[:, 8:16], values))
                link(nc.vector.max_index(where[:, 8:16], best[:, 8:16], values))

            def lookup(b, which):
                eq = selA.rearrange("p h k a -> p (h k) a")
                link(tt(eq, abf[:, which, b, :].unsqueeze(2).to_broadcast([P, SLOTS, 16]),
                        iota[:, 0:16].unsqueeze(1).to_broadcast([P, SLOTS, 16]), ALU.is_equal))
                lists = ixf[:, b, :, :].rearrange("p (h w) a -> p h w a", w=2)[:, :, which, :]
                link(tt(selA, selA, lists.unsqueeze(2).to_broadcast([P, 8, 16, 16]), ALU.mult))
                link(nc.vector.tensor_reduce(isel[:, which, b, :], eq, AX_X, ALU.add))

            for j in range(HALF):
                n = u_first(0) + j
                lo_dve(n + 2, n % 2)
                if j < 32:
                    b, m = j // 16, j % 16
                    top16(sc_all[:, b, m, :], v16[:, b, m, :], ix16[:, b, m, :])
                elif j < 48:
                    b, h = (j - 32) // 8, (j - 32) % 8
                    link(tt(cand.rearrange("p (a c) -> p a c", a=16), v16[:, b, 2 * h, :].unsqueeze(2).to_broadcast([P, 16, 16]),
                            v16[:, b, 2 * h + 1, :].unsqueeze(1).to_broadcast([P, 16, 16]), ALU.add))
                    top16(cand, pick[:, b, h, :], ci[:, b, 16 * h:16 * h + 16])
                elif j == 48:
                    link(nc.vector.tensor_copy(ixf, ix16))
                    nc.vector.tensor_single_scalar(cab[:, 0, :, :], ci, 4, ALU.logical_shift_right)
                    link(nc.vector.tensor_single_scalar(cab[:, 1, :, :], ci, 15, ALU.bitwise_and))
                    link(nc.vector.tensor_copy(abf, cab))
                    link(nc.vector.tensor_copy(gsum, pick[:, :, :, 0]))
                    tt(pick, pick, gsum.unsqueeze(3).to_broadcast([P, TB, 8, 16]), ALU.subtract).then_inc(pick_shift, 1)
                elif j < 53:
                    lookup((j - 49) // 2, (j - 49) % 2)
            dve.wait_ge(pick_exp, 1)
            link(nc.vector.tensor_reduce(gsum, pick, AX_X, ALU.add))
            link(nc.vector.reciprocal(gsum, gsum))
            tt(pick, pick, gsum.unsqueeze(3).to_broadcast([P, TB, 8, 16]), ALU.mult).then_inc(slots_ready, 1)

            def apply_group(i, s, half):
                g = i * 2 + (half * GROUPS + s)
                dve.wait_ge(g_psum, g + 1)
                at = acts[:, :, bass.ds(i * (2 * GT) + s * GT, GT)].rearrange("p j t -> p t j")
                tt(at, at, bank[2 + s][:, :].rearrange("p (t j) -> p t j", t=GT), ALU.mult).then_inc(g_applied, 1)

            def one_hots(i, s, half):
                t0 = i * (2 * GT) + s * GT
                tt(oh2[:, s, :, :], iota[:, half * HALF:(half + 1) * HALF].unsqueeze(1).to_broadcast([P, GT, HALF]),
                   slotT[:, 1, bass.ds(t0, GT)].unsqueeze(2).to_broadcast([P, GT, HALF]), ALU.is_equal).then_inc(oh2_eq, 1)
                tt(oh1[:, s, :, :], iota.unsqueeze(1).to_broadcast([P, GT, P]),
                   slotT[:, 0, bass.ds(t0, GT)].unsqueeze(2).to_broadcast([P, GT, P]), ALU.is_equal).then_inc(oh1_done, 1)

            for half in range(2):
                if half == 1:
                    with dve.Fori(0, HALF // 2) as i:
                        for s in range(2):
                            n0 = u_first(1) + 2 + s
                            lo_dve(i * 2 + n0, n0 % 2)
                dve.wait_ge(slots_evac, 3)
                dve.wait_ge(gelu_done, HALF * (half + 1))
                for s in range(2):
                    one_hots(0, s, half)
                with dve.Fori(0, GROUPS // 2 - 1) as i:
                    for s in range(2):
                        apply_group(i, s, half)
                        one_hots(i + 1, s, half)
                for s in range(2):
                    g = half * GROUPS + GROUPS - 2 + s
                    dve.wait_ge(g_psum, g + 1)
                    t0 = S - 2 * GT + s * GT
                    at = acts[:, :, t0:t0 + GT].rearrange("p j t -> p t j")
                    tt(at, at, bank[2 + s][:, :].rearrange("p (t j) -> p t j", t=GT), ALU.mult).then_inc(g_applied, 1)
                for s in range(2):
                    dve.wait_ge(ah_done, half * HALF + s + 1)
                    tt(al[:, s, :], acts[:, s, :], ah[:, s, :].bitcast(F32), ALU.subtract).then_inc(al_done, 1)
                with dve.Fori(0, HALF // 2 - 1) as i:
                    for s in range(2):
                        n0 = v_first(half) + 2 + s
                        lo_dve(i * 2 + n0, n0 % 2)
                        dve.wait_ge(ah_done, i * 2 + (half * HALF + s + 3))
                        tt(al[:, s, :], acts[:, bass.ds(i * 2 + (s + 2), 1), :].rearrange("p o t -> p (o t)"),
                           ah[:, s, :].bitcast(F32), ALU.subtract).then_inc(al_done, 1)
                if half == 0:
                    for s in range(2):
                        n = u_first(1) + s
                        lo_dve(n, n % 2)
                dve.wait_ge(pe_used, v_first(half) + HALF)
                for b in range(TB):
                    for q in range(4):
                        r = resid[:, b, q * C:(q + 1) * C]
                        tt(r, r, bank[4 * b + q][:, :], ALU.add).then_inc(v_added, 1)

        @block.tensor
        def _(pe):
            def unit_there(n):
                pe.wait_ge(hi_done, n + 1)
                pe.wait_ge(lo_dve_done, n + 1)
                pe.wait_ge(lo_pool_done, n + 1)

            def transpose_rows(src):
                for k in range(KT):
                    for b in range(TB):
                        ins = nc.tensor.transpose(bank[k // 2][:, (k % 2) * S + b * P:(k % 2) * S + (b + 1) * P],
                                                  src[:, b, k * P:(k + 1) * P], ident)
                    if k % 2:
                        ins.then_inc(xt_psum, 1)

            def project(n, banks, k0, nk, w):
                slot = n % 2
                unit_there(n)
                for k in range(nk):
                    wh, wl = hi[:, slot, k * w:(k + 1) * w], lo[:, slot, k * w:(k + 1) * w]
                    for b in range(TB):
                        xh, xl = (XT[:, k0 + k, part, b * P:(b + 1) * P] for part in range(2))
                        first, last = k0 + k == 0, k0 + k == KT - 1
                        o = bank[banks + b][:, 0:w]
                        nc.tensor.matmul(o, xh, wh, start=first, stop=False)
                        nc.tensor.matmul(o, xh, wl, start=False, stop=False)
                        ins = nc.tensor.matmul(o, xl, wh, start=False, stop=last)
                ins.then_inc(pe_used, 1)

            def transpose_chunk(t):
                c = TR_CHUNKS[t]
                pe.wait_ge(z_ready, t + 1)
                if t >= 1:
                    pe.wait_ge(tr_evac, t)
                if CHUNKS[c][0] == "ki":
                    for b in range(TB):
                        ins = nc.tensor.transpose(bank[4][:, b * P:(b + 1) * P], kidup[:, b, :], ident)
                else:
                    for q in range(4):
                        for b in range(TB):
                            ins = nc.tensor.transpose(bank[4 + q // 2][:, (q % 2) * S + b * P:(q % 2) * S + (b + 1) * P],
                                                      zt[:, c % 2, b, q * P:(q + 1) * P], ident)
                ins.then_inc(tr_psum, 1)

            def index_scores(g):
                b, pairs = g // 4, (2 * (g % 4), 2 * (g % 4) + 1)
                if g >= 1:
                    pe.wait_ge(idx_relu, g)
                if g == 0:
                    pe.wait_ge(tr_evac, 3)
                for j, pair in enumerate(pairs):
                    for h in range(2):
                        rows = slice(64 * h, 64 * h + 64)
                        ins = nc.tensor.matmul(bank[6 + h][:, j * S:(j + 1) * S], qiT[rows, pair, b * P:(b + 1) * P],
                                               kiT[rows, :], start=True, stop=True)
                ins.then_inc(idx_psum, 1)

            pe.wait_ge(const_in, 16 * N_CONST)
            pe.wait_ge(rows_scaled, 1)
            transpose_rows(xs)
            pe.wait_ge(xt_lo, KT)
            for c, (name, _, w) in enumerate(CHUNKS):
                if c == NZ:
                    pe.wait_ge(rows_scaled, 2)
                    pe.wait_ge(z_evac, NZ)
                    pe.wait_ge(tr_evac, 8)
                    pe.wait_ge(idx_relu, 8)
                    transpose_rows(ms)
                    pe.wait_ge(xt_lo, 2 * KT)
                if c >= 2:
                    pe.wait_ge(z_evac, c - 1)
                for u in range(UNITS_OF[c]):
                    nk = KT // UNITS_OF[c]
                    project(FIRST_OF[c] + u, 2 * (c % 2), u * nk, nk, w)
                if c - 1 in TR_CHUNKS:
                    transpose_chunk(TR_CHUNKS.index(c - 1))
                if c in IDX_AT:
                    for g in range(IDX_AT[c], IDX_AT[c] + 2):
                        index_scores(g)
            pe.wait_ge(poolm_in, 16)
            for g in range(4):
                for b in range(TB):
                    ins = nc.tensor.matmul(bank[6 + g // 2][:, (g % 2) * S:(g % 2 + 1) * S], pu_sb[:, b, g * P:(g + 1) * P],
                                           poolM[:, g, b, :], start=(b == 0), stop=(b == TB - 1))
                if g % 2:
                    ins.then_inc(poold_psum, 1)
            pe.wait_ge(z_evac, len(CHUNKS))
            pe.wait_ge(tr_evac, len(TR_CHUNKS))
            for i in range(HEADS + 2):
                if i < HEADS:
                    if i >= 2:
                        pe.wait_ge(logit_masked, i - 1)
                    ql, kl = (qT[:, i, :], kT[:, i, :]) if i < A_HEADS else (qmT[:, i - 8, :], kmT[:, i - 8, :])
                    for b in range(TB):
                        ins = nc.tensor.matmul(bank[i % 2][:, b * S:(b + 1) * S], ql[:, b * P:(b + 1) * P], kl,
                                               start=True, stop=True)
                    ins.then_inc(logit_psum, 1)
                if 0 <= i - 1 < HEADS:
                    h = i - 1
                    pe.wait_ge(prob_ready, h + 1)
                    if h >= 2:
                        pe.wait_ge(probT_evac, h - 1)
                    for sb_ in range(TB):
                        for b in range(TB):
                            ins = nc.tensor.transpose(bank[2 + h % 2][:, sb_ * S + b * P:sb_ * S + (b + 1) * P],
                                                      prob[:, h % 2, b, sb_ * P:(sb_ + 1) * P], ident)
                    ins.then_inc(probT_psum, 1)
                if i == 1:
                    for g in range(4):
                        pe.wait_ge(poold_evac, 2)
                        ins = nc.tensor.matmul(bank[6 + g // 2][:, (g % 2) * S:(g % 2 + 1) * S], poolW[:, g, :],
                                               pooldT[:, g, :], start=True, stop=True)
                        if g % 2:
                            ins.then_inc(poolw_psum, 1)
                if i >= 2:
                    h = i - 2
                    pe.wait_ge(probT_evac, h + 1)
                    if h >= 2:
                        pe.wait_ge(xt_lo, 36 + h - 1)
                    for sb_ in range(TB):
                        vv = v_sb[:, sb_, h * P:(h + 1) * P] if h < A_HEADS else vm_sb[:, sb_, (h - 8) * P:(h - 7) * P]
                        ins = nc.tensor.matmul(bank[4 + h % 2][:, 0:S], vv, probT[:, h % 2, sb_, :],
                                               start=(sb_ == 0), stop=(sb_ == TB - 1))
                    ins.then_inc(av_psum, 1)
            pe.wait_ge(xt_lo, 48)
            for oc in range(4):
                if oc >= 2:
                    pe.wait_ge(h_added, oc - 1)
                for u in range(4):
                    project(N_OUT + 4 * oc + u, 2 * (oc % 2), 4 * u, 4, C)
            pe.wait_ge(h_added, 4)
            pe.wait_ge(rows_scaled, 3)
            transpose_rows(hs)
            pe.wait_ge(xt_lo, 64)

            def expert_products(slot, b):
                for k in range(KT):
                    wh, wl = hi[:, slot, k * P:(k + 1) * P], lo[:, slot, k * P:(k + 1) * P]
                    o = bank[b][:, 0:S]
                    nc.tensor.matmul(o, wh, XT[:, k, 0, :], start=(k == 0), stop=False)
                    nc.tensor.matmul(o, wh, XT[:, k, 1, :], start=False, stop=False)
                    ins = nc.tensor.matmul(o, wl, XT[:, k, 0, :], start=False, stop=(k == KT - 1))
                ins.then_inc(pe_used, 1)

            for m in range(17):
                if m < 16:
                    n = N_WQ + m
                    unit_there(n)
                    if m >= 2:
                        pe.wait_ge(wq_evac, m - 1)
                    expert_products(n % 2, m % 2)
                if m >= 1:
                    pe.wait_ge(wq_evac, m)
                    if m >= 3:
                        pe.wait_ge(key_evac, m - 2)
                    for b in range(TB):
                        ins = nc.tensor.matmul(bank[4 + (m - 1) % 2][:, b * P:(b + 1) * P],
                                               qTr[:, (m - 1) % 2, b * P:(b + 1) * P], keysT[:, (m - 1) % 2, :],
                                               start=True, stop=True)
                    ins.then_inc(key_psum, 1)
            for half in range(2):
                n0 = u_first(half)
                if half == 1:
                    pe.wait_ge(v_added, 2)
                for s in range(2):
                    unit_there(n0 + s)
                    expert_products((n0 + s) % 2, (n0 + s) % 2)
                with pe.Fori(1, HALF // 2) as i:
                    for s in range(2):
                        unit_there(i * 2 + (n0 + s))
                        pe.wait_ge(gelu_done, i * 2 + (half * HALF + s - 1))
                        expert_products((n0 + s) % 2, (n0 + s) % 2)
                if half == 0:
                    pe.wait_ge(slots_ready, 1)
                    pe.wait_ge(key_evac, 16)
                    for x in range(3):
                        for b in range(TB):
                            src = isel[:, x, b, :] if x < 2 else pick[:, b, :, :].rearrange("p h k -> p (h k)")
                            ins = nc.tensor.transpose(bank[4 + x][:, b * P:(b + 1) * P], src, ident)
                        ins.then_inc(slots_psum, 1)
                else:
                    pe.wait_ge(v_added, 8)
                with pe.Fori(0, GROUPS // 2) as i:
                    for s in range(2):
                        g = i * 2 + (half * GROUPS + s)
                        pe.wait_ge(oh1_done, g + 1)
                        pe.wait_ge(oh2_done, g + 1)
                        for t in range(GT):
                            ins = nc.tensor.matmul(bank[2 + s][:, t * HALF:(t + 1) * HALF], oh1[:, s, t, :], oh2[:, s, t, :],
                                                   start=True, stop=True)
                        ins.then_inc(g_psum, 1)
                pe.wait_ge(g_applied, GROUPS * (half + 1))
                n0 = v_first(half)

                def v_products(n, slot, s, first, last):
                    unit_there(n)
                    for b in range(TB):
                        xh, xl = ah[:, s, b * P:(b + 1) * P], al[:, s, b * P:(b + 1) * P]
                        for q in range(4):
                            vh, vl = hi[:, slot, q * C:(q + 1) * C], lo[:, slot, q * C:(q + 1) * C]
                            o = bank[4 * b + q][:, :]
                            nc.tensor.matmul(o, xh, vh, start=first, stop=False, skip_group_check=True)
                            nc.tensor.matmul(o, xh, vl, start=False, stop=False, skip_group_check=True)
                            ins = nc.tensor.matmul(o, xl, vh, start=False, stop=last, skip_group_check=True)
                    ins.then_inc(pe_used, 1)

                pe.wait_ge(al_done, half * HALF + 1)
                v_products(n0, n0 % 2, 0, True, False)
                pe.wait_ge(al_done, half * HALF + 2)
                v_products(n0 + 1, (n0 + 1) % 2, 1, False, False)
                with pe.Fori(1, HALF // 2 - 1) as i:
                    for s in range(2):
                        pe.wait_ge(al_done, i * 2 + (half * HALF + s + 1))
                        v_products(i * 2 + (n0 + s), (n0 + s) % 2, s, False, False)
                pe.wait_ge(al_done, half * HALF + HALF - 1)
                v_products(n0 + HALF - 2, n0 % 2, 0, False, False)
                pe.wait_ge(al_done, half * HALF + HALF)
                v_products(n0 + HALF - 1, (n0 + 1) % 2, 1, False, True)


def constants():
    pos = np.arange(S, dtype=np.float32)

    def rope(half):
        inv = (np.float32(10000.0) ** (-np.arange(half, dtype=np.float32) / np.float32(half))).astype(np.float32)
        ang = (pos[:, None] * inv[None, :]).astype(np.float32)
        t = np.stack([np.cos(ang), np.sin(ang)]).astype(np.float32)
        return np.ascontiguousarray(t.reshape(2, TB, P, half).transpose(2, 0, 1, 3))

    main = np.zeros((P, 256), np.float32)
    main[:, 0:128] = np.eye(P)
    main[:, 128:256] = np.arange(P)[None, :]
    chunk = np.arange(S) // 64
    adm = np.where(chunk[None, :] <= chunk[:, None], 0.0, NOT_ADMISSIBLE).astype(np.float32)
    adm = np.ascontiguousarray(adm.reshape(TB, P, S).transpose(1, 0, 2))
    pool = np.zeros((4, S, S), np.float32)
    for g, w in enumerate((2, 4, 8, 16)):
        for t in range(S):
            lo_ = max(t + 1 - w, 0)
            pool[g, lo_:t + 1, t] = np.float32(1.0) / np.float32(t + 1 - lo_)
            pool[g, t, t] -= 1.0
    pool = np.ascontiguousarray(pool.reshape(4, TB, P, S).transpose(2, 0, 1, 3))
    return main, adm, pool, rope(64).reshape(P, -1), rope(32).reshape(P, -1)


def units(w, width):
    n = w.shape[1] // width
    k = UNIT // width
    t = w.reshape(KT // k, k, P, n, width)
    return t.transpose(3, 0, 2, 1, 4).reshape(n * (KT // k), P, k * width)


def kernel(**inputs):
    import concourse.bacc as bacc
    from concourse.bass_utils import run_bass_kernel_spmd as run

    x = {k: np.asarray(v) for k, v in inputs.items()}
    w_in = x["w_in"][0]
    w_mix = np.concatenate([units(w_in[:, f:f + w], C) for name, f, w in Z_CHUNKS if name != "ki"]
                           + [units(x["w_mem_kv"][0], C), units(x["w_out"][0], C), units(x["peer_w_q"][0], P)])
    _, f, w = Z_CHUNKS[2]
    main, adm, pool, rope_a, rope_i = constants()
    arrays = {
        "x": x["x"][0], "mem": x["mem"][0], "w_mix": w_mix,
        "w_ki": w_in[:, f:f + w].reshape(KT, P, w).transpose(1, 0, 2).reshape(P, KT * w),
        "c_main": np.concatenate([main, x["peer_sub_keys_1"][0].T, x["peer_sub_keys_2"][0].T]
                                 + [x[g][0].reshape(KT, P).T for g in ("attn_norm_gain", "mem_norm_gain", "ffn_norm_gain")]
                                 + [x["pool_scale"][0].reshape(4, P).T], axis=1),
        "c_mix": np.concatenate([np.broadcast_to(x[g][0], (P, P)) for g in
                                 ("q_norm_gain", "k_norm_gain", "mq_norm_gain", "mk_norm_gain")]
                                + [rope_a, rope_i, x["pool_w"][0].transpose(1, 0, 2).reshape(P, 4 * P)], axis=1),
        "c_adm": adm, "c_pool": pool,
        "u": x["peer_u"][0].reshape(P, P, KT, P).transpose(1, 3, 2, 0).reshape(P, P, KT * P),
        "v": x["peer_v"][0].reshape(P, P, D),
    }
    arrays = {k: np.ascontiguousarray(v) for k, v in arrays.items()}
    nc = bacc.Bacc("TRN2", target_bir_lowering=False, num_devices=1)
    aps = {n: nc.dram_tensor(f"in_{n}", v.shape, F32, kind="ExternalInput").ap() for n, v in arrays.items()}
    out = nc.dram_tensor("out_h", (S, D), F32, kind="ExternalOutput").ap()
    build(nc, aps, out)
    r = run(nc, [{f"in_{n}": v for n, v in arrays.items()}], core_ids=[0])
    return r.results[0]["out_h"].reshape(1, S, D)
```

```python
from contextlib import ExitStack

import concourse.bass as bass
from concourse import mybir
import numpy as np

F32 = mybir.dt.float32
F32R = mybir.dt.float32r
U32 = mybir.dt.uint32
ALU = mybir.AluOpType
ACT = mybir.ActivationFunctionType
AX_X = mybir.AxisListType.X

P = 128
D = 2048
S = 256
TB = S // P
KT = D // P
EPS = 1e-6
A_HEADS, M_HEADS, IDX_HEADS = 8, 4, 16
UNIT = 2048
C = 512
CHUNKS = [("km", 0, 0, C), ("vm", 0, 512, C),
          ("qm", 1, 4688, C), ("qi", 1, 3072, C), ("qi", 1, 3584, C), ("ki", 1, 4096, 80), ("q", 1, 0, C),
          ("k", 1, 1024, C), ("q", 1, 512, C), ("k", 1, 1536, C), ("v", 1, 2048, C), ("v", 1, 2560, C),
          ("pu", 1, 4176, C)]
NC = len(CHUNKS)
UNITS_OF = [4 if ch[3] == C else 1 for ch in CHUNKS]
FIRST_OF = [sum(UNITS_OF[:c]) for c in range(NC + 1)]
CHUNK_OF = [c for c in range(NC) for _ in range(UNITS_OF[c])]
N_X = FIRST_OF[2]
N_KI = FIRST_OF[5]
N_OUT = FIRST_OF[-1]
N_WQ = N_OUT + 16
N_EXP = N_WQ + 16
QTR = 32
QUARTERS = P // QTR
N_ALL = N_EXP + 2 * QUARTERS * QTR

NORMED = [c for c in range(NC) if CHUNKS[c][0] in ("q", "k", "qm", "km")]
TR_CHUNKS = [c for c in range(NC) if CHUNKS[c][0] in ("qi", "ki", "q", "k", "qm", "km")]
TR_STEPS = sorted((FIRST_OF[c + 1] + 2 + part, c, part) for c in TR_CHUNKS for part in range(2)
                  if not (CHUNKS[c][0] == "ki" and part == 0))
TR_AT = {slot: t for t, (slot, _, _) in enumerate(TR_STEPS)}
TR_DONE = {(c, part): t + 1 for t, (_, c, part) in enumerate(TR_STEPS)}
IDX_AT = {26 + g: g for g in range(8)}
TOP_AT = (35, 36, 37, 38)
HEAD_SLOTS = [16 + i for i in range(M_HEADS)] + [39 + i for i in range(A_HEADS)]
HEADS = len(HEAD_SLOTS)
LOGIT_AT = {x: i for i, x in enumerate(HEAD_SLOTS)}
PROBT_AT = {x + 1: i for i, x in enumerate(HEAD_SLOTS)}
AV_AT = {x + 2: i for i, x in enumerate(HEAD_SLOTS)}
XSQ_SLOT = 2

PEER_HEADS, PEER_K = 8, 16
SLOTS = PEER_HEADS * PEER_K
GT = 8
GROUPS = S // GT
EXP_TILE = 10
ROUTE = 16
ADD_ORDER = (1, 0, 2, 3, 4, 5, 6, 7)
NOT_ADMISSIBLE = -1e38
TAKEN = -3e38
ATT_SCALE = 128.0 ** -0.5
IDX_SCALE = 64.0 ** -0.5


def u_first(q):
    return N_EXP + 2 * QTR * q


def v_first(q):
    return u_first(q) + QTR


def pool_share(n):
    return 1536 if N_OUT + 2 <= n < N_EXP + ROUTE + 2 else 1024


def build(nc, a, out):
    with ExitStack() as ctx:
        def sb(name, shape, dt=F32):
            return ctx.enter_context(nc.sbuf_tensor(name, shape, dt))

        def sem(name):
            return ctx.enter_context(nc.semaphore(name))

        resid = sb("resid", [P, TB, D])
        big = sb("big", [P, 2 * QTR * S])
        XT = sb("XT", [P, KT, 2, S], F32R)
        raw = sb("raw", [P, 2, UNIT])
        hi = sb("hi", [P, 2, UNIT], F32R)
        lo = sb("lo", [P, 2, UNIT], F32R)
        ah = sb("ah", [P, 2, S], F32R)
        al = sb("al", [P, 2, S], F32R)
        oh1 = sb("oh1", [P, 2, GT, P], F32R)
        oh2 = sb("oh2", [P, 2, GT, 2, QTR], F32R)
        scr = sb("scr", [P, 7168])
        cst = sb("cst", [P, 592])
        ident, iota = cst[:, 0:128], cst[:, 128:256]
        keysT = cst[:, 256:512].rearrange("p (s n) -> p s n", s=2)
        gains = cst[:, 512:512 + 3 * KT].rearrange("p (r k) -> p r k", r=3)
        pscale = cst[:, 560:564]
        ssq = cst[:, 564:572].rearrange("p (b o) -> p b o", b=TB)
        var = cst[:, 572:574]
        rstd = cst[:, 574:580].rearrange("p (r b) -> p r b", r=3)
        ssum = cst[:, 580:582]

        xs = big[:, 0:4096].rearrange("p (b d) -> p b d", b=TB)
        v_sb = big[:, 0:2048].rearrange("p (b d) -> p b d", b=TB)
        pu_sb = big[:, 2048:3072].rearrange("p (b d) -> p b d", b=TB)
        vm_sb = big[:, 3072:4096].rearrange("p (b d) -> p b d", b=TB)
        ms = big[:, 4096:8192].rearrange("p (b d) -> p b d", b=TB)
        prob = big[:, 4096:5120].rearrange("p (r b s) -> p r b s", r=2, b=TB)
        relu = big[:, 4096:5120].rearrange("p (h j s) -> p h j s", h=2, j=2)
        probT = big[:, 5120:6144].rearrange("p (r b s) -> p r b s", r=2, b=TB)
        poolM = big[:, 6144:8192].rearrange("p (g b t) -> p g b t", g=4, b=TB)
        qT = big[:, 8192:10240].rearrange("p (h t) -> p h t", h=8)
        kT = big[:, 10240:12288].rearrange("p (h t) -> p h t", h=8)
        qiT = big[:, 12288:14336].rearrange("p (h t) -> p h t", h=8)
        qmT = big[:, 14336:15360].rearrange("p (h t) -> p h t", h=4)
        kmT = big[:, 15360:16384].rearrange("p (h t) -> p h t", h=4)
        hs = big[:, 12288:16384].rearrange("p (b d) -> p b d", b=TB)
        zt = scr[:, 0:2048].rearrange("p (r b d) -> p r b d", r=2, b=TB)
        pooldT = scr[:, 0:1024].rearrange("p (g t) -> p g t", g=4)
        tmpA = scr[:, 2048:3072]
        tmpB = scr[:, 3072:4096]
        score = scr[:, 4096:4608].rearrange("p (b s) -> p b s", b=TB)
        mbias = scr[:, 4608:5120].rearrange("p (b s) -> p b s", b=TB)
        kiT = scr[:, 5120:5376]
        kidup = scr[:, 5376:5632].rearrange("p (b d) -> p b d", b=TB)
        wi = scr[:, 5632:5664].rearrange("p (b h) -> p b h", b=TB)
        top8 = scr[:, 5664:5672]
        hstat = scr[:, 5672:5696].rearrange("p (n h) -> p n h", n=3)
        astat = scr[:, 5696:5712].rearrange("p (r n b) -> p r n b", r=2, n=4)
        hgain = scr[:, 5760:6272].rearrange("p (n d) -> p n d", n=4)
        ropeA = scr[:, 6272:6528].rearrange("p (n b f) -> p n b f", n=2, b=TB)
        ropeI = scr[:, 6528:6656].rearrange("p (n b f) -> p n b f", n=2, b=TB)
        poolW = scr[:, 6656:7168].rearrange("p (g e) -> p g e", g=4)
        def mixed_of(i):
            return qmT[:, i, :] if i < M_HEADS else qT[:, i - M_HEADS, :]

        acts = big[:, 0:QTR * S].rearrange("p (j t) -> p j t", j=QTR)
        gts = big[:, QTR * S:2 * QTR * S]
        gts_tj = gts.rearrange("p (t j) -> p t j", j=QTR)
        comb = scr[:, 256:768].rearrange("p (r t) -> p r t", r=2)
        prod = scr[:, 768:1280].rearrange("p (r t) -> p r t", r=2)
        isel = scr[:, 1280:1792].rearrange("p (n b s) -> p n b s", n=2, b=TB)
        pick = scr[:, 1792:2048].rearrange("p (b h k) -> p b h k", b=TB, h=8)
        i1T, i2T = scr[:, 2048:2304], scr[:, 2304:2560]
        gT = scr[:, 2560:3072].rearrange("p (n t) -> p n t", n=2)
        gsum = scr[:, 3072:3088].rearrange("p (b h) -> p b h", b=TB)
        r0 = QTR * S
        keysc = big[:, r0:r0 + 512].rearrange("p (r b n) -> p r b n", r=2, b=TB)
        v16 = big[:, r0 + 512:r0 + 1024].rearrange("p (b m a) -> p b m a", b=TB, m=16)
        ix16 = big[:, r0 + 1024:r0 + 1536].bitcast(U32).rearrange("p (b m a) -> p b m a", b=TB, m=16)
        ixf = big[:, r0 + 1536:r0 + 2048].rearrange("p (b m a) -> p b m a", b=TB, m=16)
        cand = big[:, r0 + 2048:r0 + 2304]
        ci = big[:, r0 + 2304:r0 + 2560].bitcast(U32).rearrange("p (b s) -> p b s", b=TB)
        cab = big[:, r0 + 2560:r0 + 3072].bitcast(U32).rearrange("p (n b s) -> p n b s", n=2, b=TB)
        abf = big[:, r0 + 3072:r0 + 3584].rearrange("p (n b s) -> p n b s", n=2, b=TB)
        selA = big[:, r0 + 4096:r0 + 6144].rearrange("p (h k a) -> p h k a", h=8, k=16)

        bank = [ctx.enter_context(nc.psum_tensor(f"bank{i}", [P, 512], F32)) for i in range(8)]

        const_in = sem("const_in")
        x_in = sem("x_in")
        mem_in = [sem(f"mem_in{i}") for i in range(4)]
        mixc_in = sem("mixc_in")
        poolm_in = sem("poolm_in")
        raw_in = [sem("raw_in0"), sem("raw_in1")]
        hi_done = sem("hi_done")
        lo_dve_done = sem("lo_dve_done")
        lo_pool_done = sem("lo_pool_done")
        pe_used = sem("pe_used")
        ssq_done = sem("ssq_done")
        var_done = sem("var_done")
        std_done = sem("std_done")
        rstd_done = sem("rstd_done")
        rows_scaled = sem("rows_scaled")
        xt_psum = sem("xt_psum")
        xt_hi = sem("xt_hi")
        xt_lo = sem("xt_lo")
        z_evac = sem("z_evac")
        z_ready = sem("z_ready")
        hvar_done = sem("hvar_done")
        hstd_done = sem("hstd_done")
        tr_psum = sem("tr_psum")
        tr_evac = sem("tr_evac")
        idx_psum = sem("idx_psum")
        idx_relu = sem("idx_relu")
        idx_added = sem("idx_added")
        poold_psum = sem("poold_psum")
        poold_evac = sem("poold_evac")
        poolw_psum = sem("poolw_psum")
        logit_psum = sem("logit_psum")
        logit_masked = sem("logit_masked")
        prob_exp = sem("prob_exp")
        prob_ready = sem("prob_ready")
        probT_psum = sem("probT_psum")
        probT_evac = sem("probT_evac")
        av_psum = sem("av_psum")
        av_evac = sem("av_evac")
        h_added = sem("h_added")
        comb_done = sem("comb_done")
        key_psum = sem("key_psum")
        key_evac = sem("key_evac")
        gelu_done = sem("gelu_done")
        pick_shift = sem("pick_shift")
        pick_exp = sem("pick_exp")
        slots_ready = sem("slots_ready")
        slots_psum = sem("slots_psum")
        slots_evac = sem("slots_evac")
        gsplit_done = sem("gsplit_done")
        oh1_done = sem("oh1_done")
        oh2_done = sem("oh2_done")
        oh2_eq = sem("oh2_eq")
        g_psum = sem("g_psum")
        g_evac = sem("g_evac")
        prod_done = sem("prod_done")
        ah_done = sem("ah_done")
        al_done = sem("al_done")
        v_added = sem("v_added")
        out_done = sem("out_done")
        dve_step = sem("dve_step")

        block = ctx.enter_context(nc.Block())

        def xt_before(r):
            return KT * r

        @block.sync
        def _(sp):
            def load_unit(n, slot, src):
                if not (isinstance(n, int) and n < 2):
                    sp.wait_ge(hi_done, n - 1)
                    sp.wait_ge(lo_dve_done, n - 1)
                    sp.wait_ge(lo_pool_done, n - 1)
                sp.dma_start(raw[:, slot, 0:src.shape[-1]], src).then_inc(raw_in[slot], 16)

            sp.dma_start(cst[:, 0:564], a["c_main"]).then_inc(const_in, 16)
            for i in range(4):
                cols = slice(i * C, (i + 1) * C)
                sp.dma_start(ms[:, :, cols], a["mem"].rearrange("(b p) d -> p b d", p=P)[:, :, cols])                    .then_inc(mem_in[i], 16)
            for n in range(N_EXP):
                load_unit(n, n % 2, a["w_ki"] if n == N_KI else a["w_mix"][n - (n > N_KI)])
                if n == 1:
                    sp.dma_start(scr[:, 5760:7168], a["c_mix"]).then_inc(mixc_in, 16)
                    sp.dma_start(score, a["c_adm"]).then_inc(mixc_in, 16)
                    sp.dma_start(resid[:, :, :], a["x"].rearrange("(b p) d -> p b d", p=P)).then_inc(x_in, 16)
            for q in range(QUARTERS):
                n0 = u_first(q)
                with sp.Fori(0, QTR // 2) as i:
                    for s in range(2):
                        load_unit(i * 2 + (n0 + s), (n0 + s) % 2,
                                  a["u"][bass.ds(i * 2 + (q * QTR + s), 1), :, :].rearrange("o p f -> p (o f)"))
                n0 = v_first(q)
                with sp.Fori(0, QTR // 2) as i:
                    for s in range(2):
                        load_unit(i * 2 + (n0 + s), (n0 + s) % 2,
                                  a["v"][:, bass.ds(i * 2 + (q * QTR + s), 1), :].rearrange("p o f -> p (o f)"))
            for i, x in enumerate(ADD_ORDER):
                b, c = x // 4, x % 4
                sp.wait_ge(v_added, 8 * (QUARTERS - 1) + i + 1)
                sp.dma_start(out[b * P:(b + 1) * P, c * C:(c + 1) * C], resid[:, b, c * C:(c + 1) * C])\
                    .then_inc(out_done, 16)
            sp.wait_ge(out_done, 16 * 4 * TB)

        @block.gpsimd
        def _(pool):
            def lo_pool(n, slot, share):
                pool.wait_ge(hi_done, n + 1)
                if not (isinstance(n, int) and n < 2):
                    pool.wait_ge(pe_used, n - 1)
                nc.gpsimd.tensor_tensor(lo[:, slot, 0:share], raw[:, slot, 0:share], hi[:, slot, 0:share].bitcast(F32),
                                        ALU.subtract).then_inc(lo_pool_done, 1)

            def lo_pool_range(first, end):
                with pool.Fori(0, (end - first) // 2) as i:
                    for s in range(2):
                        lo_pool(i * 2 + (first + s), (first + s) % 2, pool_share(first))

            def weigh(g_abs, t0, s):
                pool.wait_ge(oh2_eq, g_abs + 1)
                o = oh2[:, s, :, :, :]
                nc.gpsimd.tensor_tensor(o, o, gT[:, :, bass.ds(t0, GT)].rearrange("p n t -> p t n").unsqueeze(3)
                                        .to_broadcast([P, GT, 2, QTR]), ALU.mult).then_inc(oh2_done, 1)

            lo_pool(0, 0, pool_share(0))
            lo_pool(1, 1, pool_share(1))
            lo_pool_range(2, 10)
            pool.wait_ge(xt_psum, 8)
            pool.dma_start(poolM, a["c_pool"]).then_inc(poolm_in, 16)
            lo_pool_range(10, N_OUT + 1)
            lo_pool(N_OUT + 1, (N_OUT + 1) % 2, pool_share(N_OUT + 1))
            lo_pool_range(N_OUT + 2, N_EXP + ROUTE + 2)
            pool.wait_ge(gsplit_done, 1)
            for s in range(2):
                weigh(s, s * GT, s)
            with pool.Fori(0, (QTR - ROUTE) // 2 - 1) as i:
                for s in range(2):
                    n = N_EXP + ROUTE + 2 + s
                    lo_pool(i * 2 + n, n % 2, pool_share(n))
                    for r in range(2):
                        weigh(i * 4 + (2 * s + r + 2), i * (4 * GT) + (2 * s + r + 2) * GT, r)
            for s in range(2):
                n = N_EXP + QTR + s
                lo_pool(n, n % 2, pool_share(n))
                if s == 0:
                    for g in range(GROUPS - 2, GROUPS):
                        weigh(g, g * GT, g % 2)
            for q in range(QUARTERS):
                if q >= 1:
                    for s in range(2):
                        weigh(q * GROUPS + s, s * GT, s)
                    n0 = u_first(q) + 2
                    with pool.Fori(0, QTR // 2 - 1) as i:
                        for s in range(2):
                            lo_pool(i * 2 + (n0 + s), (n0 + s) % 2, pool_share(n0))
                            weigh(i * 2 + (q * GROUPS + s + 2), i * (2 * GT) + (s + 2) * GT, s)
                    for s in range(2):
                        n = n0 + QTR - 2 + s
                        lo_pool(n, n % 2, pool_share(n))
                n0 = v_first(q) + 2
                lo_pool_range(n0, n0 + QTR if q < QUARTERS - 1 else N_ALL)

        @block.scalar
        def _(act):
            def make_hi(n):
                act.wait_ge(raw_in[n % 2], 16 * (n // 2 + 1))
                if n >= 2:
                    act.wait_ge(pe_used, n - 1)
                nc.scalar.activation(hi[:, n % 2, :], raw[:, n % 2, :], ACT.Copy).then_inc(hi_done, 1)

            def make_hi_loop(i, n0):
                act.wait_ge(raw_in[n0 % 2], i * 16 + 16 * (n0 // 2 + 1))
                act.wait_ge(pe_used, i * 2 + (n0 - 1))
                nc.scalar.activation(hi[:, n0 % 2, :], raw[:, n0 % 2, :], ACT.Copy).then_inc(hi_done, 1)

            def square(src, junk, b, o):
                return nc.scalar.activation(junk, src, ACT.Square, accum_out=ssq[:, b, o:o + 1])

            def row_std(r):
                act.wait_ge(var_done, r + 1)
                nc.scalar.activation(rstd[:, r, :], var, ACT.Sqrt).then_inc(std_done, 1)

            def xt_high(psum_round, xt_round, gain):
                for k in range(KT):
                    act.wait_ge(xt_psum, 8 * psum_round + k // 2 + 1)
                    src = bank[4 + k // 2 % 4][:, (k % 2) * S:(k % 2 + 1) * S]
                    nc.scalar.activation(XT[:, k, 0, :], src, ACT.Copy, scale=gains[:, gain, k:k + 1]).then_inc(xt_hi, 1)

            def evac_chunk(c):
                name, _, first, w = CHUNKS[c]
                act.wait_ge(pe_used, FIRST_OF[c + 1])
                dst = {"pu": pu_sb, "vm": vm_sb}.get(name, zt[:, c % 2])
                if name == "v":
                    dst = v_sb[:, :, first - 2048:first - 2048 + C]
                elif name not in ("pu", "vm"):
                    earlier = [x for x in TR_CHUNKS if x < c and x % 2 == c % 2]
                    if earlier:
                        act.wait_ge(tr_psum, TR_DONE[earlier[-1], 1])
                act.wait_ge(rstd_done, CHUNKS[c][1] + 1)
                for b in range(TB):
                    ins = nc.scalar.activation(dst[:, b, 0:w], bank[2 * (c % 2) + b][:, 0:w], ACT.Copy,
                                               scale=rstd[:, CHUNKS[c][1], b:b + 1])
                ins.then_inc(z_evac, 1)

            def head_std(c):
                act.wait_ge(hvar_done, NORMED.index(c) + 1)
                nc.scalar.activation(hstat[:, 2, :], hstat[:, 1, :], ACT.Sqrt).then_inc(hstd_done, 1)

            def evac_transposed(t):
                _, c, part = TR_STEPS[t]
                name, _, first, _ = CHUNKS[c]
                act.wait_ge(tr_psum, t + 1)
                if name == "ki":
                    nc.scalar.activation(kiT, bank[4][:, 0:S], ACT.Copy).then_inc(tr_evac, 1)
                    return
                dst = {"qi": qiT, "q": qT, "k": kT, "qm": qmT, "km": kmT}[name]
                at = (4 * (first // C % 2) if name in ("qi", "q", "k") else 0) + 2 * part
                nc.scalar.activation(dst[:, at:at + 2, :], bank[4][:, :].rearrange("p (h t) -> p h t", h=2), ACT.Copy)\
                    .then_inc(tr_evac, 1)

            def index_relu(g):
                act.wait_ge(idx_psum, g + 1)
                if g >= 1:
                    act.wait_ge(idx_added, g)
                for h in range(2):
                    ins = nc.scalar.activation(relu[:, h, :, :], bank[6 + h][:, :].rearrange("p (j s) -> p j s", j=2),
                                               ACT.Relu, scale=IDX_SCALE)
                ins.then_inc(idx_relu, 1)

            def exponentials(i):
                act.wait_ge(logit_masked, i + 1)
                for b in range(TB):
                    ins = nc.scalar.activation(prob[:, i % 2, b, :], prob[:, i % 2, b, :], ACT.Exp,
                                               bias=astat[:, i % 2, 0, b:b + 1], accum_out=astat[:, i % 2, 1, b:b + 1])
                ins.then_inc(prob_exp, 1)

            def evac_probT(i):
                act.wait_ge(probT_psum, i + 1)
                if i >= 2:
                    act.wait_ge(av_psum, i - 1)
                nc.scalar.activation(probT[:, i % 2, :, :], bank[7][:, :].rearrange("p (b s) -> p b s", b=TB),
                                     ACT.Copy).then_inc(probT_evac, 1)

            def evac_av(i):
                act.wait_ge(av_psum, i + 1)
                nc.scalar.activation(mixed_of(i), bank[5][:, 0:S], ACT.Copy).then_inc(av_evac, 1)

            act.wait_ge(const_in, 16)
            xt_high(0, 0, 0)
            make_hi(0)
            for n in range(N_OUT + 1):
                make_hi(n + 1)
                if n - 1 in TR_AT:
                    evac_transposed(TR_AT[n - 1])
                if n == N_X:
                    xt_high(1, 1, 1)
                if n in FIRST_OF[1:]:
                    evac_chunk(FIRST_OF.index(n) - 1)
                if n - 1 in IDX_AT:
                    index_relu(IDX_AT[n - 1])
                if n - 1 in LOGIT_AT:
                    exponentials(LOGIT_AT[n - 1])
                if n - 1 in PROBT_AT:
                    evac_probT(PROBT_AT[n - 1])
                if n - 1 in AV_AT:
                    evac_av(AV_AT[n - 1])
                if n - 1 in [FIRST_OF[c + 1] for c in NORMED]:
                    head_std(FIRST_OF.index(n - 1) - 1)
                if n == 0:
                    for b in range(TB):
                        ins = square(ms[:, b, :], xs[:, b, :], b, 0)
                    ins.then_inc(ssq_done, 1)
                    row_std(0)
                if n == XSQ_SLOT:
                    act.wait_ge(x_in, 16)
                    act.wait_ge(rstd_done, 1)
                    for b in range(TB):
                        ins = square(resid[:, b, :], xs[:, b, :], b, 0)
                    ins.then_inc(ssq_done, 1)
                    row_std(1)
            for i in range(HEADS):
                k = (i - M_HEADS) if i >= M_HEADS else A_HEADS + i
                act.wait_ge(av_evac, i + 1)
                nc.scalar.activation(XT[:, k, 0, :], mixed_of(i), ACT.Copy).then_inc(xt_hi, 1)
            for g in range(2):
                act.wait_ge(poold_psum, g + 1)
                nc.scalar.activation(pooldT[:, 2 * g:2 * g + 2, :], bank[6 + g][:, :].rearrange("p (g t) -> p g t", g=2),
                                     ACT.Copy).then_inc(poold_evac, 1)
            for g in range(4):
                act.wait_ge(poolw_psum, g // 2 + 1)
                nc.scalar.activation(XT[:, 12 + g, 0, :], bank[6 + g // 2][:, (g % 2) * S:(g % 2 + 1) * S],
                                     ACT.Copy, scale=pscale[:, g:g + 1]).then_inc(xt_hi, 1)
            for oc in range(4):
                for n in range(N_OUT + 4 * oc + 2, N_OUT + 4 * oc + 6):
                    make_hi(n)
                act.wait_ge(h_added, oc + 1)
                for b in range(TB):
                    ins = square(resid[:, b, oc * C:(oc + 1) * C], hs[:, b, oc * C:(oc + 1) * C], b, oc)
            ins.then_inc(ssq_done, 1)
            row_std(2)
            xt_high(2, 3, 2)
            for m in range(17):
                if m < 16:
                    make_hi(N_WQ + m + 2)
                if m >= 1:
                    act.wait_ge(key_psum, m)
                    nc.scalar.activation(keysc[:, (m - 1) % 2, :, :],
                                         bank[4 + (m - 1) % 2][:, 0:S].rearrange("p (b n) -> p b n", b=TB), ACT.Copy)\
                        .then_inc(key_evac, 1)

            def gelu(i, j0, q):
                act.wait_ge(comb_done, i * 2 + (16 + q * QTR + j0 + 1))
                nc.scalar.activation(acts[:, bass.ds(i * 2 + j0, 1), :], comb[:, (u_first(q) + j0) % 2, :].unsqueeze(1), ACT.Gelu)\
                    .then_inc(gelu_done, 1)

            for q in range(QUARTERS):
                n0 = u_first(q)
                if q == 0:
                    for first, end in ((0, EXP_TILE), (EXP_TILE, ROUTE)):
                        with act.Fori(0, (end - first) // 2) as i:
                            for s in range(2):
                                make_hi_loop(i, n0 + first + s + 2)
                                gelu(i, first + s, 0)
                        if end == EXP_TILE:
                            act.wait_ge(pick_shift, 1)
                            nc.scalar.activation(pick, pick, ACT.Exp).then_inc(pick_exp, 1)
                    for x, dst in enumerate((i1T, i2T)):
                        act.wait_ge(slots_psum, x + 1)
                        nc.scalar.activation(dst, bank[4 + x][:, 0:S], ACT.Copy).then_inc(slots_evac, 1)
                    with act.Fori(0, (QTR - ROUTE) // 2) as i:
                        for s in range(2):
                            make_hi_loop(i, n0 + ROUTE + s + 2)
                            gelu(i, ROUTE + s, 0)
                else:
                    with act.Fori(0, QTR // 2) as i:
                        for s in range(2):
                            make_hi_loop(i, n0 + s + 2)
                            gelu(i, s, q)
                n0 = v_first(q)
                for s in range(2):
                    act.wait_ge(prod_done, q * QTR + s + 1)
                    nc.scalar.activation(ah[:, s, :], prod[:, s, :], ACT.Copy).then_inc(ah_done, 1)
                with act.Fori(0, QTR // 2 - 1) as i:
                    for s in range(2):
                        make_hi_loop(i, n0 + s + 2)
                        act.wait_ge(prod_done, i * 2 + (q * QTR + s + 3))
                        nc.scalar.activation(ah[:, s, :], prod[:, s, :], ACT.Copy).then_inc(ah_done, 1)
                if q < QUARTERS - 1:
                    for s in range(2):
                        make_hi(n0 + QTR + s)

        @block.vector
        def _(dve):
            steps = [0]

            def link(ins):
                steps[0] += 1
                ins.then_inc(dve_step, 1)
                dve.wait_ge(dve_step, steps[0])

            tt = nc.vector.tensor_tensor

            def lo_dve(n, slot, share):
                dve.wait_ge(hi_done, n + 1)
                if not (isinstance(n, int) and n < 2):
                    dve.wait_ge(pe_used, n - 1)
                tt(lo[:, slot, share:UNIT], raw[:, slot, share:UNIT], hi[:, slot, share:UNIT].bitcast(F32),
                   ALU.subtract).then_inc(lo_dve_done, 1)

            def row_rstd(r):
                dve.wait_ge(ssq_done, r + 1)
                sums = ssq[:, :, 0]
                if r == 2:
                    link(nc.vector.tensor_reduce(ssum, ssq, AX_X, ALU.add))
                    sums = ssum
                nc.vector.tensor_scalar(var, sums, 1.0 / D, EPS, ALU.mult, ALU.add).then_inc(var_done, 1)
                dve.wait_ge(std_done, r + 1)
                nc.vector.reciprocal(rstd[:, r, :], rstd[:, r, :]).then_inc(rstd_done, 1)
                dve.wait_ge(rstd_done, r + 1)

            def xt_low(xt_round, gain):
                for k in range(KT):
                    dve.wait_ge(xt_hi, xt_before(xt_round) + (k | 1) + 1)
                    src = bank[4 + k // 2 % 4][:, (k % 2) * S:(k % 2 + 1) * S]
                    nc.vector.scalar_tensor_tensor(XT[:, k, 1, :], src, gains[:, gain, k:k + 1],
                                                   XT[:, k, 0, :].bitcast(F32), ALU.mult, ALU.subtract).then_inc(xt_lo, 1)

            def heads_a(c):
                z = zt[:, c % 2].rearrange("p b (h d) -> p (b h) d", d=P)
                t = tmpA.rearrange("p (h d) -> p h d", d=P)
                dve.wait_ge(z_evac, c + 1)
                link(tt(t, z, z, ALU.mult))
                link(nc.vector.tensor_reduce(hstat[:, 0, :], t, AX_X, ALU.add))
                nc.vector.tensor_scalar(hstat[:, 1, :], hstat[:, 0, :], 1.0 / P, EPS, ALU.mult, ALU.add)\
                    .then_inc(hvar_done, 1)

            def signal_ready(ins, c):
                ins.then_inc(z_ready, 1)
                dve.wait_ge(z_ready, TR_CHUNKS.index(c) + 1)

            def heads_b(c):
                name = CHUNKS[c][0]
                dve.wait_ge(z_evac, c + 1)
                z = zt[:, c % 2]
                if c in NORMED:
                    z3 = z.rearrange("p b (h d) -> p (b h) d", d=P)
                    dve.wait_ge(hstd_done, NORMED.index(c) + 1)
                    link(nc.vector.reciprocal(hstat[:, 2, :], hstat[:, 2, :]))
                    link(tt(z3, z3, hstat[:, 2, :].unsqueeze(2).to_broadcast([P, 8, P]), ALU.mult))
                    gain = hgain[:, ("q", "k", "qm", "km").index(name), :].unsqueeze(1).to_broadcast([P, 8, P])
                    ins = tt(z3, z3, gain, ALU.mult)
                    if name in ("qm", "km"):
                        signal_ready(ins, c)
                        return
                    link(ins)
                rope = ropeA if name in ("q", "k") else ropeI
                f = 64 if name in ("q", "k") else 32
                w = 64 if name == "ki" else C
                nh = w // f
                z4 = z[:, :, 0:w].rearrange("p b (h f) -> p b h f", f=f)
                tA = tmpA[:, 0:2 * w].rearrange("p (b h f) -> p b h f", b=TB, f=f)
                tB = tmpB[:, 0:2 * w].rearrange("p (b h f) -> p b h f", b=TB, f=f)
                tt(tA, z4, rope[:, 0, :, :].unsqueeze(2).to_broadcast([P, TB, nh, f]), ALU.mult)
                link(tt(tB, z4, rope[:, 1, :, :].unsqueeze(2).to_broadcast([P, TB, nh, f]), ALU.mult))
                a5 = tmpA[:, 0:2 * w].rearrange("p (b h g f) -> p b h g f", b=TB, g=2, f=f)
                b5 = tmpB[:, 0:2 * w].rearrange("p (b h g f) -> p b h g f", b=TB, g=2, f=f)
                if name != "ki":
                    z5 = z.rearrange("p b (h g f) -> p b h g f", g=2, f=f)
                    tt(z5[:, :, :, 0, :], a5[:, :, :, 0, :], b5[:, :, :, 1, :], ALU.subtract)
                    signal_ready(tt(z5[:, :, :, 1, :], a5[:, :, :, 1, :], b5[:, :, :, 0, :], ALU.add), c)
                    return
                for copy in range(2):
                    tt(kidup[:, :, 64 * copy:64 * copy + f], a5[:, :, 0, 0, :], b5[:, :, 0, 1, :], ALU.subtract)
                    tt(kidup[:, :, 64 * copy + f:64 * copy + 2 * f], a5[:, :, 0, 1, :], b5[:, :, 0, 0, :], ALU.add)
                signal_ready(nc.vector.tensor_scalar(wi, z[:, :, 64:80], IDX_HEADS ** -0.5, None, ALU.mult), c)

            def index_add(g):
                b = g // 4
                dve.wait_ge(idx_relu, g + 1)
                for j in range(2):
                    for h in range(2):
                        head = 2 * (2 * (g % 4) + j) + h
                        ins = nc.vector.scalar_tensor_tensor(score[:, b, :], relu[:, h, j, :], wi[:, b, head:head + 1],
                                                             score[:, b, :], ALU.mult, ALU.add)
                        if (j, h) != (1, 1):
                            link(ins)
                ins.then_inc(idx_added, 1)
                dve.wait_ge(idx_added, g + 1)

            def take_eight(b):
                link(nc.vector.max(top8, score[:, b, :]))
                link(nc.vector.match_replace(score[:, b, :], top8, score[:, b, :], TAKEN))

            def softmax_head(i):
                r = i % 2
                dve.wait_ge(logit_psum, i + 1)
                if i >= 2:
                    dve.wait_ge(probT_psum, i - 1)
                src = bank[6][:, :].rearrange("p (b s) -> p b s", b=TB)
                if i >= M_HEADS:
                    link(nc.vector.scalar_tensor_tensor(prob[:, r, :, :], src, ATT_SCALE, mbias, ALU.mult, ALU.add))
                else:
                    link(nc.vector.tensor_scalar(prob[:, r, :, :], src, ATT_SCALE, None, ALU.mult))
                link(nc.vector.tensor_reduce(astat[:, r, 2, :], prob[:, r, :, :], AX_X, ALU.max))
                nc.vector.tensor_scalar(astat[:, r, 0, :], astat[:, r, 2, :], -1.0, None, ALU.mult)\
                    .then_inc(logit_masked, 1)
                dve.wait_ge(prob_exp, i + 1)
                link(nc.vector.reciprocal(astat[:, r, 3, :], astat[:, r, 1, :]))
                for b in range(TB):
                    ins = nc.vector.tensor_scalar(prob[:, r, b, :], prob[:, r, b, :], astat[:, r, 3, b:b + 1],
                                                  None, ALU.mult)
                ins.then_inc(prob_ready, 1)

            dve.wait_ge(const_in, 16)
            xt_low(0, 0)
            lo_dve(0, 0, pool_share(0))
            for n in range(N_OUT + 1):
                lo_dve(n + 1, (n + 1) % 2, pool_share(n + 1))
                if n == N_X:
                    xt_low(1, 1)
                if n in [FIRST_OF[c + 1] for c in NORMED]:
                    heads_a(FIRST_OF.index(n) - 1)
                if n - 1 in IDX_AT:
                    index_add(IDX_AT[n - 1])
                if n in TOP_AT:
                    for _ in range(4):
                        take_eight(TOP_AT.index(n) // 2)
                if n == TOP_AT[-1] + 1:
                    for b in range(TB):
                        link(nc.vector.tensor_scalar(mbias[:, b, :], score[:, b, :], 0.5 * (TAKEN + NOT_ADMISSIBLE),
                                                     -1e30, ALU.is_gt, ALU.mult))
                if n - 1 in LOGIT_AT:
                    softmax_head(LOGIT_AT[n - 1])
                if n - 1 in [FIRST_OF[c + 1] for c in TR_CHUNKS]:
                    heads_b(FIRST_OF.index(n - 1) - 1)
                if n == 0:
                    row_rstd(0)
                if n == XSQ_SLOT:
                    row_rstd(1)
                    dve.wait_ge(mixc_in, 32)
            for i in range(HEADS):
                k = (i - M_HEADS) if i >= M_HEADS else A_HEADS + i
                dve.wait_ge(xt_hi, xt_before(2) + i + 1)
                tt(XT[:, k, 1, :], mixed_of(i), XT[:, k, 0, :].bitcast(F32), ALU.subtract).then_inc(xt_lo, 1)
            for g in range(4):
                dve.wait_ge(xt_hi, xt_before(2) + HEADS + (g | 1) + 1)
                nc.vector.scalar_tensor_tensor(XT[:, 12 + g, 1, :], bank[6 + g // 2][:, (g % 2) * S:(g % 2 + 1) * S],
                                               pscale[:, g:g + 1], XT[:, 12 + g, 0, :].bitcast(F32),
                                               ALU.mult, ALU.subtract).then_inc(xt_lo, 1)
            for oc in range(4):
                for n in range(N_OUT + 4 * oc + 2, N_OUT + 4 * oc + 6):
                    lo_dve(n, n % 2, pool_share(n))
                dve.wait_ge(pe_used, N_OUT + 4 * oc + 4)
                for b in range(TB):
                    r = resid[:, b, oc * C:(oc + 1) * C]
                    ins = tt(r, r, bank[2 * (oc % 2) + b][:, :], ALU.add)
                ins.then_inc(h_added, 1)
            row_rstd(2)
            for b in range(TB):
                ins = nc.vector.tensor_scalar(hs[:, b, :], resid[:, b, :], rstd[:, 2, b:b + 1], None, ALU.mult)
            ins.then_inc(rows_scaled, 1)
            xt_low(3, 2)

            def top16(values, best, where):
                link(nc.vector.max(best[:, 0:8], values))
                link(nc.vector.max_index(where[:, 0:8], best[:, 0:8], values))
                link(nc.vector.match_replace(values, best[:, 0:8], values, TAKEN))
                link(nc.vector.max(best[:, 8:16], values))
                link(nc.vector.max_index(where[:, 8:16], best[:, 8:16], values))

            def add_halves(b):
                nc.vector.tensor_reduce(comb[:, b, :], bank[b][:, :].rearrange("p (n t) -> p t n", n=2), AX_X, ALU.add)\
                    .then_inc(comb_done, 1)

            def combine_query(m):
                if m >= 2:
                    dve.wait_ge(key_psum, m - 1)
                dve.wait_ge(pe_used, N_WQ + m + 1)
                add_halves((N_WQ + m) % 2)

            def combine_tile(j, q, b):
                if not (isinstance(j, int) and q == 0 and j < 2):
                    dve.wait_ge(gelu_done, j + (q * QTR - 1))
                dve.wait_ge(pe_used, j + (u_first(q) + 1))
                add_halves(b)

            def best_of_keys(m, b):
                top16(keysc[:, m % 2, b, :], v16[:, b, m, :], ix16[:, b, m, :])

            def best_of_pairs(b, h):
                link(tt(cand.rearrange("p (a c) -> p a c", a=16), v16[:, b, 2 * h, :].unsqueeze(2).to_broadcast([P, 16, 16]),
                        v16[:, b, 2 * h + 1, :].unsqueeze(1).to_broadcast([P, 16, 16]), ALU.add))
                top16(cand, pick[:, b, h, :], ci[:, b, 16 * h:16 * h + 16])

            for m in range(17):
                n = N_WQ + m
                if m < 16:
                    combine_query(m)
                if m >= 1:
                    dve.wait_ge(key_evac, m)
                    best_of_keys(m - 1, 0)
                if m < 16:
                    lo_dve(n + 2, n % 2, pool_share(n + 2))
                if m >= 1:
                    best_of_keys(m - 1, 1)
                if m >= 4 and m % 2 == 0:
                    best_of_pairs(0, m // 2 - 2)

            def positions(b):
                link(nc.vector.tensor_copy(ixf[:, b, :, :], ix16[:, b, :, :]))
                nc.vector.tensor_single_scalar(cab[:, 0, b, :], ci[:, b, :], 4, ALU.logical_shift_right)
                link(nc.vector.tensor_single_scalar(cab[:, 1, b, :], ci[:, b, :], 15, ALU.bitwise_and))
                link(nc.vector.tensor_copy(abf[:, :, b, :], cab[:, :, b, :]))

            def lookup(b, step):
                which, step = step // 3, step % 3
                eq = selA.rearrange("p h k a -> p (h k) a")
                if step == 0:
                    ins = tt(eq, abf[:, which, b, :].unsqueeze(2).to_broadcast([P, SLOTS, 16]),
                             iota[:, 0:16].unsqueeze(1).to_broadcast([P, SLOTS, 16]), ALU.is_equal)
                elif step == 1:
                    lists = ixf[:, b, :, :].rearrange("p (h w) a -> p h w a", w=2)[:, :, which, :]
                    ins = tt(selA, selA, lists.unsqueeze(2).to_broadcast([P, 8, 16, 16]), ALU.mult)
                else:
                    ins = nc.vector.tensor_reduce(isel[:, which, b, :], eq, AX_X, ALU.add)
                link(ins)

            def take_weights(g_abs, t0, s):
                dve.wait_ge(g_psum, g_abs + 1)
                nc.vector.tensor_reduce(gts[:, bass.ds(t0 * QTR, GT * QTR)].rearrange("p (t j) -> p t j", j=QTR),
                                        bank[2 + s][:, :].rearrange("p (t n j) -> p t j n", t=GT, n=2), AX_X, ALU.add)\
                    .then_inc(g_evac, 1)

            def one_hots(t0, s, q):
                tt(oh2[:, s, :, :, :], iota[:, q * QTR:(q + 1) * QTR].unsqueeze(1).unsqueeze(1).to_broadcast([P, GT, 2, QTR]),
                   i2T[:, bass.ds(t0, GT)].unsqueeze(2).unsqueeze(3).to_broadcast([P, GT, 2, QTR]),
                   ALU.is_equal).then_inc(oh2_eq, 1)
                tt(oh1[:, s, :, :], iota.unsqueeze(1).to_broadcast([P, GT, P]),
                   i1T[:, bass.ds(t0, GT)].unsqueeze(2).to_broadcast([P, GT, P]), ALU.is_equal).then_inc(oh1_done, 1)

            for j in range(ROUTE):
                n = N_EXP + j
                combine_tile(j, 0, n % 2)
                if j == 0:
                    best_of_pairs(0, 7)
                    positions(0)
                elif j < 9:
                    best_of_pairs(1, j - 1)
                lo_dve(n + 2, n % 2, pool_share(n + 2))
                if 1 <= j < 7:
                    lookup(0, j - 1)
                if j == 9:
                    link(nc.vector.tensor_copy(gsum, pick[:, :, :, 0]))
                    tt(pick, pick, gsum.unsqueeze(3).to_broadcast([P, TB, 8, 16]), ALU.subtract).then_inc(pick_shift, 1)
                    positions(1)
                if 10 <= j < 16:
                    lookup(1, j - 10)
                if j == 14:
                    dve.wait_ge(pick_exp, 1)
                    link(nc.vector.tensor_reduce(gsum, pick, AX_X, ALU.add))
                    link(nc.vector.reciprocal(gsum, gsum))
                    link(tt(pick, pick, gsum.unsqueeze(3).to_broadcast([P, TB, 8, 16]), ALU.mult))
            nc.vector.tensor_copy(gsum, gsum).then_inc(slots_ready, 1)
            dve.wait_ge(slots_psum, 3)
            link(nc.vector.tensor_copy(gT[:, 0, :].bitcast(F32R), bank[6][:, 0:S]))
            tt(gT[:, 1, :], bank[6][:, 0:S], gT[:, 0, :], ALU.subtract).then_inc(gsplit_done, 1)
            dve.wait_ge(slots_evac, 2)
            for s in range(2):
                one_hots(s * GT, s, 0)
            with dve.Fori(0, (QTR - ROUTE) // 2 - 1) as i:
                for s in range(2):
                    n = N_EXP + ROUTE + s
                    combine_tile(i * 2 + (ROUTE + s), 0, n % 2)
                    lo_dve(i * 2 + (n + 2), n % 2, pool_share(n + 2))
                    for r in range(2):
                        take_weights(i * 4 + (2 * s + r), i * (4 * GT) + (2 * s + r) * GT, r)
                        one_hots(i * (4 * GT) + (2 * s + r + 2) * GT, r, 0)
            for s in range(2):
                n = N_EXP + QTR - 2 + s
                combine_tile(QTR - 2 + s, 0, n % 2)
                lo_dve(n + 2, n % 2, pool_share(n + 2))
                for r in range(2):
                    g = GROUPS - 4 + 2 * s + r
                    take_weights(g, g * GT, r)
                    if s == 0:
                        one_hots((g + 2) * GT, r, 0)

            for q in range(QUARTERS):
                if q >= 1:
                    for s in range(2):
                        one_hots(s * GT, s, q)
                    n0 = u_first(q)
                    with dve.Fori(0, QTR // 2 - 1) as i:
                        for s in range(2):
                            combine_tile(i * 2 + s, q, (n0 + s) % 2)
                            lo_dve(i * 2 + (n0 + s + 2), (n0 + s) % 2, pool_share(n0))
                            take_weights(i * 2 + (q * GROUPS + s), i * (2 * GT) + s * GT, s)
                            one_hots(i * (2 * GT) + (s + 2) * GT, s, q)
                    for s in range(2):
                        n = n0 + QTR - 2 + s
                        combine_tile(QTR - 2 + s, q, n % 2)
                        lo_dve(n + 2, n % 2, pool_share(n0))
                        g = GROUPS - 2 + s
                        take_weights(q * GROUPS + g, g * GT, s)

                def weighted(j, s):
                    if not isinstance(j, int):
                        j = bass.ds(j, 1)
                        x, g = acts[:, j, :].rearrange("p o t -> p (o t)"), gts_tj[:, :, j].rearrange("p t o -> p (t o)")
                    else:
                        x, g = acts[:, j, :], gts_tj[:, :, j]
                    tt(prod[:, s, :], x, g, ALU.mult).then_inc(prod_done, 1)

                def weighted_low(count, s):
                    dve.wait_ge(ah_done, count)
                    tt(al[:, s, :], prod[:, s, :], ah[:, s, :].bitcast(F32), ALU.subtract).then_inc(al_done, 1)

                dve.wait_ge(g_evac, (q + 1) * GROUPS)
                dve.wait_ge(gelu_done, q * QTR + 2)
                for s in range(2):
                    weighted(s, s)
                for s in range(2):
                    weighted_low(q * QTR + s + 1, s)
                dve.wait_ge(gelu_done, (q + 1) * QTR)
                n0 = v_first(q)
                with dve.Fori(0, QTR // 2 - 1) as i:
                    for s in range(2):
                        dve.wait_ge(al_done, i * 2 + (q * QTR + s + 1))
                        weighted(i * 2 + (s + 2), s)
                        lo_dve(i * 2 + (n0 + s + 2), (n0 + s) % 2, pool_share(n0))
                        weighted_low(i * 2 + (q * QTR + s + 3), s)
                if q < QUARTERS - 1:
                    for s in range(2):
                        n = n0 + QTR + s
                        lo_dve(n, n % 2, pool_share(n))
                dve.wait_ge(pe_used, n0 + QTR)
                for x in ADD_ORDER:
                    r = resid[:, x // 4, (x % 4) * C:(x % 4 + 1) * C]
                    tt(r, r, bank[x][:, :], ALU.add).then_inc(v_added, 1)

        @block.tensor
        def _(pe):
            def unit_there(n):
                pe.wait_ge(hi_done, n + 1)
                pe.wait_ge(lo_dve_done, n + 1)
                pe.wait_ge(lo_pool_done, n + 1)

            def transpose_rows(src, xt_round):
                for k in range(KT):
                    g = k // 2
                    if xt_round == 0 and k % 4 == 0:
                        pe.wait_ge(mem_in[k // 4], 16)
                    if k % 2 == 0 and g >= 4:
                        pe.wait_ge(xt_lo, xt_before(xt_round) + 2 * (g - 4) + 2)
                    for b in range(TB):
                        ins = nc.tensor.transpose(bank[4 + g % 4][:, (k % 2) * S + b * P:(k % 2) * S + (b + 1) * P],
                                                  src[:, b, k * P:(k + 1) * P], ident)
                    if k % 2:
                        ins.then_inc(xt_psum, 1)

            def project(n, banks, k0, nk, w, xt_round=None):
                slot = n % 2
                unit_there(n)
                for k in range(nk):
                    if xt_round is not None:
                        pe.wait_ge(xt_lo, xt_before(xt_round) + k0 + k + 1)
                    wh, wl = hi[:, slot, k * w:(k + 1) * w], lo[:, slot, k * w:(k + 1) * w]
                    for b in range(TB):
                        xh, xl = (XT[:, k0 + k, part, b * P:(b + 1) * P] for part in range(2))
                        first, last = k0 + k == 0, k0 + k == KT - 1
                        o = bank[banks + b][:, 0:w]
                        nc.tensor.matmul(o, xh, wh, start=first, stop=False)
                        nc.tensor.matmul(o, xh, wl, start=False, stop=False)
                        ins = nc.tensor.matmul(o, xl, wh, start=False, stop=last)
                ins.then_inc(pe_used, 1)

            def transpose_heads(t):
                _, c, part = TR_STEPS[t]
                pe.wait_ge(z_ready, TR_CHUNKS.index(c) + 1)
                if t >= 1:
                    pe.wait_ge(tr_evac, t)
                for b in range(TB):
                    if CHUNKS[c][0] == "ki":
                        ins = nc.tensor.transpose(bank[4][:, b * P:(b + 1) * P], kidup[:, b, :], ident)
                        continue
                    for x in range(2):
                        d = (2 * part + x) * P
                        ins = nc.tensor.transpose(bank[4][:, x * S + b * P:x * S + (b + 1) * P],
                                                  zt[:, c % 2, b, d:d + P], ident)
                ins.then_inc(tr_psum, 1)

            def index_scores(g):
                b, pairs = g // 4, (2 * (g % 4), 2 * (g % 4) + 1)
                if g >= 1:
                    pe.wait_ge(idx_relu, g)
                pe.wait_ge(tr_evac, TR_DONE[5, 1])
                for j, pair in enumerate(pairs):
                    for h in range(2):
                        rows = slice(64 * h, 64 * h + 64)
                        ins = nc.tensor.matmul(bank[6 + h][:, j * S:(j + 1) * S], qiT[rows, pair, b * P:(b + 1) * P],
                                               kiT[rows, :], start=True, stop=True)
                ins.then_inc(idx_psum, 1)

            def logits(i):
                if i >= 1:
                    pe.wait_ge(logit_masked, i)
                if i == 0:
                    pe.wait_ge(tr_evac, TR_DONE[2, 1])
                if i == M_HEADS:
                    pe.wait_ge(idx_relu, 8)
                if i >= M_HEADS:
                    pe.wait_ge(tr_evac, TR_DONE[7 if i < M_HEADS + 4 else 9, 1])
                ql = mixed_of(i)
                kl = kmT[:, i, :] if i < M_HEADS else kT[:, i - M_HEADS, :]
                for b in range(TB):
                    ins = nc.tensor.matmul(bank[6][:, b * S:(b + 1) * S], ql[:, b * P:(b + 1) * P], kl,
                                           start=True, stop=True)
                ins.then_inc(logit_psum, 1)

            def transpose_probs(i):
                pe.wait_ge(prob_ready, i + 1)
                if i >= 1:
                    pe.wait_ge(probT_evac, i)
                for k in range(TB):
                    for b in range(TB):
                        ins = nc.tensor.transpose(bank[7][:, k * S + b * P:k * S + (b + 1) * P],
                                                  prob[:, i % 2, b, k * P:(k + 1) * P], ident)
                ins.then_inc(probT_psum, 1)

            def times_v(i):
                pe.wait_ge(probT_evac, i + 1)
                if i >= 1:
                    pe.wait_ge(av_evac, i)
                h = i - M_HEADS
                pe.wait_ge(z_evac, 2 if i < M_HEADS else 11 if h < 4 else 12)
                for k in range(TB):
                    vv = vm_sb[:, k, i * P:(i + 1) * P] if h < 0 else v_sb[:, k, h * P:(h + 1) * P]
                    ins = nc.tensor.matmul(bank[5][:, 0:S], vv, probT[:, i % 2, k, :], start=(k == 0), stop=(k == TB - 1))
                ins.then_inc(av_psum, 1)

            pe.wait_ge(const_in, 16)
            transpose_rows(ms, 0)
            for n in range(N_OUT):
                c = CHUNK_OF[n]
                if n == N_X:
                    pe.wait_ge(x_in, 16)
                    pe.wait_ge(tr_evac, TR_DONE[0, 1])
                    transpose_rows(resid, 1)
                if n == FIRST_OF[c] and c >= 2:
                    pe.wait_ge(z_evac, c - 1)
                u, nk = n - FIRST_OF[c], KT // UNITS_OF[c]
                project(n, 2 * (c % 2), u * nk, nk, CHUNKS[c][3], 0 if c == 0 else 1 if c == 2 else None)
                if n in TR_AT:
                    transpose_heads(TR_AT[n])
                if n in IDX_AT:
                    index_scores(IDX_AT[n])
                if n in LOGIT_AT:
                    logits(LOGIT_AT[n])
                if n in PROBT_AT:
                    transpose_probs(PROBT_AT[n])
                if n in AV_AT:
                    times_v(AV_AT[n])
            pe.wait_ge(poolm_in, 16)
            pe.wait_ge(z_evac, NC)
            pe.wait_ge(probT_evac, HEADS)
            for g in range(4):
                for b in range(TB):
                    ins = nc.tensor.matmul(bank[6 + g // 2][:, (g % 2) * S:(g % 2 + 1) * S], pu_sb[:, b, g * P:(g + 1) * P],
                                           poolM[:, g, b, :], start=(b == 0), stop=(b == TB - 1))
                if g % 2:
                    ins.then_inc(poold_psum, 1)
            for oc in range(4):
                if oc >= 2:
                    pe.wait_ge(h_added, oc - 1)
                for u in range(4):
                    if oc == 0 and u == 1:
                        pe.wait_ge(poold_evac, 2)
                        for g in range(4):
                            ins = nc.tensor.matmul(bank[6 + g // 2][:, (g % 2) * S:(g % 2 + 1) * S], poolW[:, g, :],
                                                   pooldT[:, g, :], start=True, stop=True)
                            if g % 2:
                                ins.then_inc(poolw_psum, 1)
                    if oc == 0 and u < 3:
                        pe.wait_ge(xt_lo, xt_before(2) + (8, 12, 12)[u])
                    if oc == 0 and u == 3:
                        pe.wait_ge(xt_lo, xt_before(3))
                    project(N_OUT + 4 * oc + u, 2 * (oc % 2), 4 * u, 4, C)
            pe.wait_ge(rows_scaled, 1)
            transpose_rows(hs, 3)

            def expert_products(slot, b, xt_round=None):
                for k in range(KT):
                    if xt_round is not None:
                        pe.wait_ge(xt_lo, xt_before(xt_round) + k + 1)
                    wh, wl = hi[:, slot, k * P:(k + 1) * P], lo[:, slot, k * P:(k + 1) * P]
                    nc.tensor.matmul(bank[b][:, :], wh, XT[:, k, :, :].rearrange("p n t -> p (n t)"),
                                     start=(k == 0), stop=False, skip_group_check=True)
                    ins = nc.tensor.matmul(bank[b][:, 0:S], wl, XT[:, k, 0, :], start=False, stop=(k == KT - 1),
                                           skip_group_check=True)
                ins.then_inc(pe_used, 1)

            for m in range(17):
                if m < 16:
                    n = N_WQ + m
                    unit_there(n)
                    if m >= 2:
                        pe.wait_ge(comb_done, m - 1)
                    else:
                        pe.wait_ge(h_added, 4)
                    expert_products(n % 2, n % 2, 3 if m == 0 else None)
                if m >= 1:
                    pe.wait_ge(comb_done, m)
                    if m >= 3:
                        pe.wait_ge(key_evac, m - 2)
                    for b in range(TB):
                        ins = nc.tensor.matmul(bank[4 + (m - 1) % 2][:, b * P:(b + 1) * P],
                                               comb[:, (N_WQ + m - 1) % 2, b * P:(b + 1) * P], keysT[:, (m - 1) % 2, :],
                                               start=True, stop=True)
                    ins.then_inc(key_psum, 1)

            def tile(j, q, n0):
                unit_there(j + u_first(q))
                pe.wait_ge(comb_done, j + (16 + q * QTR - 1))
                expert_products(n0 % 2, n0 % 2)

            def group(g_abs, s):
                pe.wait_ge(oh1_done, g_abs + 1)
                pe.wait_ge(oh2_done, g_abs + 1)
                if not (isinstance(g_abs, int) and g_abs < 2):
                    pe.wait_ge(g_evac, g_abs - 1)
                for t in range(GT):
                    ins = nc.tensor.matmul(bank[2 + s][:, 2 * t * QTR:2 * (t + 1) * QTR], oh1[:, s, t, :],
                                           oh2[:, s, t, :, :].rearrange("p n j -> p (n j)"), start=True, stop=True)
                ins.then_inc(g_psum, 1)

            def v_products(n, slot, s, first, last):
                unit_there(n)
                for b in range(TB):
                    xh, xl = ah[:, s, b * P:(b + 1) * P], al[:, s, b * P:(b + 1) * P]
                    for c in range(4):
                        vh, vl = hi[:, slot, c * C:(c + 1) * C], lo[:, slot, c * C:(c + 1) * C]
                        o = bank[4 * b + c][:, :]
                        nc.tensor.matmul(o, xh, vh, start=first, stop=False, skip_group_check=True)
                        nc.tensor.matmul(o, xh, vl, start=False, stop=False, skip_group_check=True)
                        ins = nc.tensor.matmul(o, xl, vh, start=False, stop=last, skip_group_check=True)
                ins.then_inc(pe_used, 1)

            for q in range(QUARTERS):
                n0 = u_first(q)
                if q == 0:
                    with pe.Fori(0, ROUTE // 2) as i:
                        for s in range(2):
                            tile(i * 2 + s, 0, n0 + s)
                    pe.wait_ge(slots_ready, 1)
                    pe.wait_ge(key_evac, 16)
                    for x in range(3):
                        for b in range(TB):
                            src = isel[:, x, b, :] if x < 2 else pick[:, b, :, :].rearrange("p h k -> p (h k)")
                            ins = nc.tensor.transpose(bank[4 + x][:, b * P:(b + 1) * P], src, ident)
                        ins.then_inc(slots_psum, 1)
                    tile(ROUTE, 0, n0 + ROUTE)
                    for r in range(2):
                        group(r, r)
                    tile(ROUTE + 1, 0, n0 + ROUTE + 1)
                    for r in range(2):
                        group(2 + r, r)
                    with pe.Fori(1, (QTR - ROUTE) // 2) as i:
                        for s in range(2):
                            tile(i * 2 + (ROUTE + s), 0, n0 + ROUTE + s)
                            for r in range(2):
                                group(i * 4 + (2 * s + r), r)
                else:
                    for s in range(2):
                        pe.wait_ge(v_added, 8 * (q - 1) + s + 1)
                        tile(s, q, n0 + s)
                        pe.wait_ge(v_added, 8 * (q - 1) + s + 3)
                        group(q * GROUPS + s, s)
                    with pe.Fori(1, QTR // 2) as i:
                        for s in range(2):
                            tile(i * 2 + s, q, n0 + s)
                            group(i * 2 + (q * GROUPS + s), s)
                    pe.wait_ge(v_added, 8 * q)
                pe.wait_ge(comb_done, 16 + (q + 1) * QTR)
                pe.wait_ge(g_evac, (q + 1) * GROUPS)
                n0 = v_first(q)
                for s in range(2):
                    pe.wait_ge(al_done, q * QTR + s + 1)
                    v_products(n0 + s, (n0 + s) % 2, s, s == 0, False)
                with pe.Fori(1, QTR // 2 - 1) as i:
                    for s in range(2):
                        pe.wait_ge(al_done, i * 2 + (q * QTR + s + 1))
                        v_products(i * 2 + (n0 + s), (n0 + s) % 2, s, False, False)
                for s in range(2):
                    pe.wait_ge(al_done, (q + 1) * QTR - 1 + s)
                    n = n0 + QTR - 2 + s
                    v_products(n, n % 2, s, False, s == 1)


def constants():
    pos = np.arange(S, dtype=np.float32)

    def rope(half):
        inv = (np.float32(10000.0) ** (-np.arange(half, dtype=np.float32) / np.float32(half))).astype(np.float32)
        ang = (pos[:, None] * inv[None, :]).astype(np.float32)
        t = np.stack([np.cos(ang), np.sin(ang)]).astype(np.float32)
        return np.ascontiguousarray(t.reshape(2, TB, P, half).transpose(2, 0, 1, 3))

    main = np.zeros((P, 256), np.float32)
    main[:, 0:128] = np.eye(P)
    main[:, 128:256] = np.arange(P)[None, :]
    chunk = np.arange(S) // 64
    adm = np.where(chunk[None, :] <= chunk[:, None], 0.0, NOT_ADMISSIBLE).astype(np.float32)
    adm = np.ascontiguousarray(adm.reshape(TB, P, S).transpose(1, 0, 2))
    pool = np.zeros((4, S, S), np.float32)
    for g, w in enumerate((2, 4, 8, 16)):
        for t in range(S):
            lo_ = max(t + 1 - w, 0)
            pool[g, lo_:t + 1, t] = np.float32(1.0) / np.float32(t + 1 - lo_)
            pool[g, t, t] -= 1.0
    pool = np.ascontiguousarray(pool.reshape(4, TB, P, S).transpose(2, 0, 1, 3))
    return main, adm, pool, rope(64).reshape(P, -1), rope(32).reshape(P, -1)


def units(w, width):
    n = w.shape[1] // width
    k = UNIT // width
    t = w.reshape(KT // k, k, P, n, width)
    return t.transpose(3, 0, 2, 1, 4).reshape(n * (KT // k), P, k * width)


def kernel(**inputs):
    import concourse.bacc as bacc
    from concourse.bass_utils import run_bass_kernel_spmd as run

    x = {k: np.asarray(v) for k, v in inputs.items()}
    w_in = x["w_in"][0]
    w_out = x["w_out"][0]
    w_out = np.concatenate([w_out[0:1024], w_out[1536:2048], w_out[1024:1536]])
    w_mix = np.concatenate([units((x["w_mem_kv"][0], w_in)[rows][:, f:f + w], C) for name, rows, f, w in CHUNKS
                            if name != "ki"] + [units(w_out, C), units(x["peer_w_q"][0], P)])
    _, _, f, w = CHUNKS[5]
    main, adm, pool, rope_a, rope_i = constants()
    arrays = {
        "x": x["x"][0], "mem": x["mem"][0], "w_mix": w_mix,
        "w_ki": w_in[:, f:f + w].reshape(KT, P, w).transpose(1, 0, 2).reshape(P, KT * w),
        "c_main": np.concatenate([main, x["peer_sub_keys_1"][0].T, x["peer_sub_keys_2"][0].T]
                                 + [x[g][0].reshape(KT, P).T for g in ("mem_norm_gain", "attn_norm_gain", "ffn_norm_gain")]
                                 + [x["pool_scale"][0].reshape(4, P).T], axis=1),
        "c_mix": np.concatenate([np.broadcast_to(x[g][0], (P, P)) for g in
                                 ("q_norm_gain", "k_norm_gain", "mq_norm_gain", "mk_norm_gain")]
                                + [rope_a, rope_i, x["pool_w"][0].transpose(1, 0, 2).reshape(P, 4 * P)], axis=1),
        "c_adm": adm, "c_pool": pool,
        "u": x["peer_u"][0].reshape(P, P, KT, P).transpose(1, 3, 2, 0).reshape(P, P, KT * P),
        "v": x["peer_v"][0].reshape(P, P, D),
    }
    arrays = {k: np.ascontiguousarray(v) for k, v in arrays.items()}
    nc = bacc.Bacc("TRN2", target_bir_lowering=False, num_devices=1)
    aps = {n: nc.dram_tensor(f"in_{n}", v.shape, F32, kind="ExternalInput").ap() for n, v in arrays.items()}
    out = nc.dram_tensor("out_h", (S, D), F32, kind="ExternalOutput").ap()
    build(nc, aps, out)
    r = run(nc, [{f"in_{n}": v for n, v in arrays.items()}], core_ids=[0])
    return r.results[0]["out_h"].reshape(1, S, D)
```

```python
from contextlib import ExitStack

import concourse.bass as bass
from concourse import mybir
import numpy as np

F32 = mybir.dt.float32
F32R = mybir.dt.float32r
U32 = mybir.dt.uint32
ALU = mybir.AluOpType
ACT = mybir.ActivationFunctionType
AX_X = mybir.AxisListType.X

P = 128
D = 2048
S = 256
TB = S // P
KT = D // P
EPS = 1e-6
A_HEADS, M_HEADS, IDX_HEADS = 8, 4, 16
UNIT = 2048
C = 512
CHUNKS = [("km", 0, 0, C), ("vm", 0, 512, C),
          ("qm", 1, 4688, C), ("qi", 1, 3072, C), ("qi", 1, 3584, C), ("ki", 1, 4096, 80), ("q", 1, 0, C),
          ("k", 1, 1024, C), ("q", 1, 512, C), ("k", 1, 1536, C), ("v", 1, 2048, C), ("v", 1, 2560, C),
          ("pu", 1, 4176, C)]
NC = len(CHUNKS)
UNITS_OF = [4 if ch[3] == C else 1 for ch in CHUNKS]
FIRST_OF = [sum(UNITS_OF[:c]) for c in range(NC + 1)]
CHUNK_OF = [c for c in range(NC) for _ in range(UNITS_OF[c])]
N_X = FIRST_OF[2]
N_KI = FIRST_OF[5]
N_OUT = FIRST_OF[-1]
N_WQ = N_OUT + 16
N_EXP = N_WQ + 16
QTR = 32
QUARTERS = P // QTR
N_ALL = N_EXP + 2 * QUARTERS * QTR

NORMED = [c for c in range(NC) if CHUNKS[c][0] in ("q", "k", "qm", "km")]
EVAC_AT = {FIRST_OF[c + 1] + (CHUNKS[c][0] == "ki"): c for c in range(NC)}
TR_CHUNKS = [c for c in range(NC) if CHUNKS[c][0] in ("qi", "ki", "q", "k", "qm", "km")]
TR_STEPS = sorted((FIRST_OF[c + 1] + 2 + part, c, part) for c in TR_CHUNKS for part in range(2)
                  if not (CHUNKS[c][0] == "ki" and part == 0))
TR_AT = {slot: t for t, (slot, _, _) in enumerate(TR_STEPS)}
TR_DONE = {(c, part): t + 1 for t, (_, c, part) in enumerate(TR_STEPS)}
IDX_AT = {26 + g: g for g in range(8)}
TOP_AT = {31 + i: i // 4 for i in range(8)}
HEAD_SLOTS = [16 + i for i in range(M_HEADS)] + [39 + i for i in range(A_HEADS)]
HEADS = len(HEAD_SLOTS)
XT_HEADS = [4, 5, 6, 7, 0, 1, 2, 3, 8, 9, 10, 11]
XT_HEADS_AT = {N_OUT - 3: range(0, 2), N_OUT - 2: range(2, 4), N_OUT - 1: range(4, 8), N_OUT: range(8, 12)}
LOGIT_AT = {x: i for i, x in enumerate(HEAD_SLOTS)}
PROBT_AT = {x + 1: i for i, x in enumerate(HEAD_SLOTS)}
AV_AT = {x + 2: i for i, x in enumerate(HEAD_SLOTS)}
SQUARE_AT = {2: (0, 0), 3: (0, 1), 5: (1, 0), 6: (1, 1)}

PEER_HEADS, PEER_K = 8, 16
SLOTS = PEER_HEADS * PEER_K
GT = 8
GROUPS = S // GT
WIDE = (QUARTERS - 1) * QTR
WIDE_BANKS = (2, 3, 5, 6)
W_PART = 1024
EXP_TILE = 10
ROUTE = 15
PAIR_AT = (7, 11)
V_BANKS = (1, 2, 3, 0, 5, 6, 7, 4)
NOT_ADMISSIBLE = -1e38
TAKEN = -3e38
ATT_SCALE = 128.0 ** -0.5
IDX_SCALE = 64.0 ** -0.5


def u_first(q):
    return N_EXP + 2 * QTR * q


def v_first(q):
    return u_first(q) + QTR


def pool_share(n):
    if N_EXP + 8 <= n < N_EXP + ROUTE + 2:
        return 1280
    return 1536 if N_OUT + 2 <= n < N_EXP + QTR + 2 else 1024


def build(nc, a, out):
    with ExitStack() as ctx:
        def sb(name, shape, dt=F32):
            return ctx.enter_context(nc.sbuf_tensor(name, shape, dt))

        def sem(name):
            return ctx.enter_context(nc.semaphore(name))

        resid = sb("resid", [P, TB, D])
        big = sb("big", [P, 2 * QTR * S])
        XT = sb("XT", [P, KT, 2, S], F32R)
        raw = sb("raw", [P, 2, UNIT])
        hi = sb("hi", [P, 2, UNIT], F32R)
        lo = sb("lo", [P, 2, UNIT], F32R)
        ah = sb("ah", [P, 2, S], F32R)
        al = sb("al", [P, 2, S], F32R)
        oh1 = sb("oh1", [P, 2, GT, P], F32R)
        oh2 = sb("oh2", [P, GT * 2 * WIDE], F32R)
        scr = sb("scr", [P, 6656])
        cst = sb("cst", [P, 592])
        ident, iota = cst[:, 0:128], cst[:, 128:256]
        keysT = cst[:, 256:512].rearrange("p (s n) -> p s n", s=2)
        gains = cst[:, 512:512 + 3 * KT].rearrange("p (r k) -> p r k", r=3)
        pscale = cst[:, 560:564]
        ssq = cst[:, 564:572].rearrange("p (b o) -> p b o", b=TB)
        var = cst[:, 572:574]
        rstd = cst[:, 574:580].rearrange("p (r b) -> p r b", r=3)
        ssum = cst[:, 580:582]
        table_junk = cst[:, 582:585]

        xs = big[:, 0:4096].rearrange("p (b d) -> p b d", b=TB)
        v_sb = big[:, 0:2048].rearrange("p (b d) -> p b d", b=TB)
        pu_sb = big[:, 2048:3072].rearrange("p (b d) -> p b d", b=TB)
        vm_sb = big[:, 3072:4096].rearrange("p (b d) -> p b d", b=TB)
        ms = big[:, 4096:8192].rearrange("p (b d) -> p b d", b=TB)
        prob = big[:, 4096:5120].rearrange("p (r b s) -> p r b s", r=2, b=TB)
        relu = big[:, 4096:5120].rearrange("p (h j s) -> p h j s", h=2, j=2)
        probT = big[:, 5120:6144].rearrange("p (r b s) -> p r b s", r=2, b=TB)
        poolM = big[:, 6144:8192].rearrange("p (g b t) -> p g b t", g=4, b=TB)
        qT = big[:, 8192:10240].rearrange("p (h t) -> p h t", h=8)
        kT = big[:, 10240:12288].rearrange("p (h t) -> p h t", h=8)
        qiT = big[:, 12288:14336].rearrange("p (h t) -> p h t", h=8)
        qmT = big[:, 14336:15360].rearrange("p (h t) -> p h t", h=4)
        kmT = big[:, 15360:16384].rearrange("p (h t) -> p h t", h=4)
        hs = big[:, 12288:16384].rearrange("p (b d) -> p b d", b=TB)
        zt = scr[:, 0:2048].rearrange("p (r b d) -> p r b d", r=2, b=TB)
        pooldT = scr[:, 0:1024].rearrange("p (g t) -> p g t", g=4)
        tmpA = scr[:, 2048:3072]
        tmpB = scr[:, 3072:4096]
        score = scr[:, 4096:4608].rearrange("p (b s) -> p b s", b=TB)
        mbias = scr[:, 4608:5120].rearrange("p (b s) -> p b s", b=TB)
        ki_z = big[0:80, 2048:2304]
        kiT = big[:, 5120:5376]
        kidup = big[:, 5376:5632].rearrange("p (b d) -> p b d", b=TB)
        wi = scr[:, 5120:5152].rearrange("p (b h) -> p b h", b=TB)
        top8 = scr[:, 5152:5160]
        hstat = scr[:, 5160:5184].rearrange("p (n h) -> p n h", n=3)
        astat = scr[:, 5184:5200].rearrange("p (r n b) -> p r n b", r=2, n=4)
        tables = scr[:, 5248:6656]
        hgain = tables[:, 0:512].rearrange("p (n d) -> p n d", n=4)
        ropeA = tables[:, 512:768].rearrange("p (n b f) -> p n b f", n=2, b=TB)
        ropeI = tables[:, 768:896].rearrange("p (n b f) -> p n b f", n=2, b=TB)
        poolW = tables[:, 896:1408].rearrange("p (g e) -> p g e", g=4)
        def tile_of(i):
            return i - M_HEADS if i >= M_HEADS else A_HEADS + i

        def mixed_of(i):
            return qmT[:, i, :] if i < M_HEADS else qT[:, i - M_HEADS, :]

        acts = big[:, 0:QTR * S].rearrange("p (j t) -> p j t", j=QTR)
        gts = big[:, QTR * S:2 * QTR * S]
        gts_tj = gts.rearrange("p (t j) -> p t j", j=QTR)
        comb = scr[:, 256:768].rearrange("p (r t) -> p r t", r=2)
        prod = scr[:, 768:1280].rearrange("p (r t) -> p r t", r=2)
        isel = scr[:, 1280:1792].rearrange("p (n b s) -> p n b s", n=2, b=TB)
        pick = scr[:, 1792:2048].rearrange("p (b h k) -> p b h k", b=TB, h=8)
        i1T, i2T = scr[:, 2048:2304], scr[:, 2304:2560]
        gT = scr[:, 2560:3072].rearrange("p (n t) -> p n t", n=2)
        eq2 = scr[:, 1280:2048]
        stage = [scr[:, 3104 + s * 768:3872 + s * 768].rearrange("p (q t j) -> p q t j", q=QUARTERS - 1, t=GT)
                 for s in range(2)]
        gsum = scr[:, 3072:3088].rearrange("p (b h) -> p b h", b=TB)
        r0 = QTR * S
        keysc = big[:, r0:r0 + 512].rearrange("p (r b n) -> p r b n", r=2, b=TB)
        v16 = big[:, r0 + 512:r0 + 1024].rearrange("p (b m a) -> p b m a", b=TB, m=16)
        ix16 = big[:, r0 + 1024:r0 + 1536].bitcast(U32).rearrange("p (b m a) -> p b m a", b=TB, m=16)
        ixf = big[:, r0 + 1536:r0 + 2048].rearrange("p (b m a) -> p b m a", b=TB, m=16)
        cand = big[:, r0 + 2048:r0 + 2560].rearrange("p (b n) -> p b n", b=TB)
        ci = big[:, r0 + 2560:r0 + 2816].bitcast(U32).rearrange("p (b s) -> p b s", b=TB)
        cab = big[:, r0 + 2816:r0 + 3328].bitcast(U32).rearrange("p (b m k) -> p b m k", b=TB, m=16)
        abf = big[:, r0 + 3328:r0 + 3840].rearrange("p (b m k) -> p b m k", b=TB, m=16)
        sel = big[:, r0 + 4096:r0 + 8192].rearrange("p (a m k) -> p a m k", a=16, m=16)

        spill = nc.dram_tensor("weights_spill", [QUARTERS - 2, P, S * QTR], F32, kind="Internal").ap()
        bank = [ctx.enter_context(nc.psum_tensor(f"bank{i}", [P, 512], F32)) for i in range(8)]

        const_in = sem("const_in")
        x_in = sem("x_in")
        mem_in = [sem(f"mem_in{i}") for i in range(4)]
        mixc_in = sem("mixc_in")
        poolm_in = sem("poolm_in")
        raw_in = [sem("raw_in0"), sem("raw_in1")]
        hi_done = sem("hi_done")
        lo_dve_done = sem("lo_dve_done")
        lo_pool_done = sem("lo_pool_done")
        pe_used = sem("pe_used")
        ssq_done = sem("ssq_done")
        var_done = sem("var_done")
        std_done = sem("std_done")
        rstd_done = sem("rstd_done")
        rows_scaled = sem("rows_scaled")
        xt_psum = sem("xt_psum")
        xt_hi = sem("xt_hi")
        xt_lo = sem("xt_lo")
        z_evac = sem("z_evac")
        ki_summed = sem("ki_summed")
        ki_psum = sem("ki_psum")
        z_ready = sem("z_ready")
        hvar_done = sem("hvar_done")
        hstd_done = sem("hstd_done")
        tr_psum = sem("tr_psum")
        tr_evac = sem("tr_evac")
        idx_psum = sem("idx_psum")
        idx_relu = sem("idx_relu")
        idx_added = sem("idx_added")
        poold_psum = sem("poold_psum")
        poold_evac = sem("poold_evac")
        poolw_psum = sem("poolw_psum")
        logit_psum = sem("logit_psum")
        logit_masked = sem("logit_masked")
        prob_exp = sem("prob_exp")
        prob_ready = sem("prob_ready")
        probT_psum = sem("probT_psum")
        probT_evac = sem("probT_evac")
        av_psum = sem("av_psum")
        av_evac = sem("av_evac")
        h_added = sem("h_added")
        comb_done = sem("comb_done")
        key_psum = sem("key_psum")
        key_evac = sem("key_evac")
        gelu_done = sem("gelu_done")
        pick_shift = sem("pick_shift")
        pick_exp = sem("pick_exp")
        slots_picked = sem("slots_picked")
        slots_psum = sem("slots_psum")
        slots_evac = sem("slots_evac")
        gsplit_done = sem("gsplit_done")
        oh1_done = sem("oh1_done")
        oh2_done = sem("oh2_done")
        oh2_eq = sem("oh2_eq")
        g_psum = sem("g_psum")
        g_evac = sem("g_evac")
        gts_copied = sem("gts_copied")
        spilled = [sem("spilled0"), sem("spilled1")]
        gts_in = sem("gts_in")
        prod_done = sem("prod_done")
        ah_done = sem("ah_done")
        al_done = sem("al_done")
        v_psum = sem("v_psum")
        v_added = sem("v_added")
        out_done = sem("out_done")
        dve_step = sem("dve_step")

        block = ctx.enter_context(nc.Block())

        def eq2_of(s, w):
            first = s * GT * QTR if w == QTR else 0
            return eq2[:, first:first + GT * w].rearrange("p (t j) -> p t j", t=GT)

        def oh2_of(s, w):
            first = s * GT * 2 * QTR if w == QTR else 0
            return oh2[:, first:first + GT * 2 * w].rearrange("p (t q n j) -> p t q n j", t=GT, n=2, j=QTR)

        def xt_before(r):
            return KT * r

        def xt_bank(r, g):
            return bank[5 + g % 3] if r == 1 else bank[4 + g % 4]


        @block.sync
        def _(sp):
            def load_unit(n, slot, src):
                if not (isinstance(n, int) and n < 2):
                    sp.wait_ge(hi_done, n - 1)
                    sp.wait_ge(lo_dve_done, n - 1)
                    sp.wait_ge(lo_pool_done, n - 1)
                sp.dma_start(raw[:, slot, 0:src.shape[-1]], src).then_inc(raw_in[slot], 16)

            def mem_part(i):
                cols = slice(i * C, (i + 1) * C)
                sp.dma_start(ms[:, :, cols], a["mem"].rearrange("(b p) d -> p b d", p=P)[:, :, cols]).then_inc(mem_in[i], 16)

            sp.dma_start(cst[:, 0:564], a["c_main"]).then_inc(const_in, 16)
            for n in range(N_EXP):
                if n < 2:
                    mem_part(n)
                load_unit(n, n % 2, a["w_ki"] if n == N_KI else a["w_mix"][n - (n > N_KI)])
                if n == 1:
                    mem_part(2)
                    mem_part(3)
                    sp.dma_start(tables, a["c_mix"]).then_inc(mixc_in, 16)
                    sp.dma_start(score, a["c_adm"]).then_inc(mixc_in, 16)
                if n == 3:
                    sp.dma_start(resid[:, :, :], a["x"].rearrange("(b p) d -> p b d", p=P)).then_inc(x_in, 16)
            for q in range(QUARTERS):
                n0 = u_first(q)
                for first, end in ((0, 4), (4, 12), (12, QTR)) if q >= 2 else ((0, QTR),):
                    if first == 4:
                        for s in range(2):
                            sp.wait_ge(spilled[s], 16 * (GROUPS // 2))
                        sp.wait_ge(prod_done, q * QTR)
                    with sp.Fori(0, (end - first) // 2) as i:
                        for s in range(2):
                            load_unit(i * 2 + (n0 + first + s), (n0 + s) % 2,
                                      a["u"][bass.ds(i * 2 + (q * QTR + first + s), 1), :, :].rearrange("o p f -> p (o f)"))
                            if first == 4:
                                cols = bass.ds(i * (2 * W_PART) + s * W_PART, W_PART)
                                sp.dma_start(gts[:, cols], spill[q - 2, :, cols]).then_inc(gts_in, 16)
                n0 = v_first(q)
                with sp.Fori(0, QTR // 2) as i:
                    for s in range(2):
                        load_unit(i * 2 + (n0 + s), (n0 + s) % 2,
                                  a["v"][:, bass.ds(i * 2 + (q * QTR + s), 1), :].rearrange("p o f -> p (o f)"))
            for i, x in enumerate(V_BANKS):
                b, c = x // 4, x % 4
                sp.wait_ge(v_added, 8 * (QUARTERS - 1) + i + 1)
                sp.dma_start(out[b * P:(b + 1) * P, c * C:(c + 1) * C], resid[:, b, c * C:(c + 1) * C])\
                    .then_inc(out_done, 16)
            sp.wait_ge(out_done, 16 * 4 * TB)

        @block.gpsimd
        def _(pool):
            def lo_pool(n, slot, share):
                pool.wait_ge(hi_done, n + 1)
                if not (isinstance(n, int) and n < 2):
                    pool.wait_ge(pe_used, n - 1)
                nc.gpsimd.tensor_tensor(lo[:, slot, 0:share], raw[:, slot, 0:share], hi[:, slot, 0:share].bitcast(F32),
                                        ALU.subtract).then_inc(lo_pool_done, 1)

            def lo_pool_range(first, end):
                with pool.Fori(0, (end - first) // 2) as i:
                    for s in range(2):
                        lo_pool(i * 2 + (first + s), (first + s) % 2, pool_share(first))

            def weigh(g_abs, t0, s, w=QTR):
                pool.wait_ge(oh2_eq, g_abs + 1)
                if w == WIDE:
                    pool.wait_ge(g_psum, g_abs)
                for k in range(w // QTR):
                    ins = nc.gpsimd.tensor_tensor(
                        oh2_of(s, w)[:, :, k, :, :],
                        eq2_of(s, w)[:, :, k * QTR:(k + 1) * QTR].unsqueeze(2).to_broadcast([P, GT, 2, QTR]),
                        gT[:, :, bass.ds(t0, GT)].rearrange("p n t -> p t n").unsqueeze(3).to_broadcast([P, GT, 2, QTR]),
                        ALU.mult)
                ins.then_inc(oh2_done, 1)

            lo_pool(0, 0, pool_share(0))
            lo_pool(1, 1, pool_share(1))
            lo_pool_range(2, 10)
            pool.wait_ge(xt_psum, 8)
            pool.dma_start(poolM, a["c_pool"]).then_inc(poolm_in, 16)
            lo_pool_range(10, N_OUT + 1)
            lo_pool(N_OUT + 1, (N_OUT + 1) % 2, pool_share(N_OUT + 1))
            lo_pool_range(N_OUT + 2, N_EXP + 8)
            lo_pool_range(N_EXP + 8, N_EXP + ROUTE + 1)
            lo_pool(N_EXP + ROUTE + 1, (N_EXP + ROUTE + 1) % 2, pool_share(N_EXP + ROUTE + 1))
            pool.wait_ge(gsplit_done, 1)
            for s in range(2):
                weigh(s, s * GT, s)
            with pool.Fori(0, (QTR - 1 - ROUTE) // 2 - 1) as i:
                for s in range(2):
                    n = N_EXP + ROUTE + 2 + s
                    lo_pool(i * 2 + n, n % 2, pool_share(n))
                    for r in range(2):
                        weigh(i * 4 + (2 * s + r + 2), i * (4 * GT) + (2 * s + r + 2) * GT, r)
            for s in range(3):
                n = N_EXP + QTR - 1 + s
                lo_pool(n, n % 2, pool_share(n))
                if s == 0:
                    for g in range(GROUPS - 2, GROUPS):
                        weigh(g, g * GT, g % 2)
            for q in range(QUARTERS):
                if q >= 1:
                    n0 = u_first(q) + 2
                    if q == 1:
                        for j in range(2):
                            weigh(GROUPS + j + 1, (j + 1) * GT, 0, WIDE)
                            lo_pool(n0 + j, (n0 + j) % 2, pool_share(n0))
                        with pool.Fori(1, QTR // 2 - 1) as i:
                            for s in range(2):
                                weigh(i * 2 + (GROUPS + s + 1), i * (2 * GT) + (s + 1) * GT, 0, WIDE)
                                lo_pool(i * 2 + (n0 + s), (n0 + s) % 2, pool_share(n0))
                        weigh(2 * GROUPS - 1, S - GT, 0, WIDE)
                        for s in range(2):
                            n = n0 + QTR - 2 + s
                            lo_pool(n, n % 2, pool_share(n))
                    else:
                        lo_pool_range(n0, n0 + QTR)
                if q == 0:
                    weigh(GROUPS, 0, 0, WIDE)
                n0 = v_first(q) + 2
                lo_pool_range(n0, n0 + QTR if q < QUARTERS - 1 else N_ALL)

        @block.scalar
        def _(act):
            def make_hi(n):
                act.wait_ge(raw_in[n % 2], 16 * (n // 2 + 1))
                if n >= 2:
                    act.wait_ge(pe_used, n - 1)
                nc.scalar.activation(hi[:, n % 2, :], raw[:, n % 2, :], ACT.Copy).then_inc(hi_done, 1)

            def make_hi_loop(i, n0):
                act.wait_ge(raw_in[n0 % 2], i * 16 + 16 * (n0 // 2 + 1))
                act.wait_ge(pe_used, i * 2 + (n0 - 1))
                nc.scalar.activation(hi[:, n0 % 2, :], raw[:, n0 % 2, :], ACT.Copy).then_inc(hi_done, 1)

            def load_table(function, i):
                nc.scalar.activation(table_junk[:, i:i + 1], ident[:, 0:1], function)

            def square(src, junk, b, o):
                return nc.scalar.activation(junk, src, ACT.Square, accum_out=ssq[:, b, o:o + 1])

            def row_std(r):
                act.wait_ge(var_done, r + 1)
                nc.scalar.activation(rstd[:, r, :], var, ACT.Sqrt).then_inc(std_done, 1)

            def xt_high(psum_round, xt_round, gain, tiles=range(KT)):
                for k in tiles:
                    act.wait_ge(xt_psum, 8 * psum_round + k // 2 + 1)
                    src = xt_bank(psum_round, k // 2)[:, (k % 2) * S:(k % 2 + 1) * S]
                    nc.scalar.activation(XT[:, k, 0, :], src, ACT.Copy, scale=gains[:, gain, k:k + 1]).then_inc(xt_hi, 1)

            def evac_chunk(c):
                name, _, first, w = CHUNKS[c]
                act.wait_ge(pe_used, FIRST_OF[c + 1])
                dst = {"pu": pu_sb, "vm": vm_sb}.get(name, zt[:, c % 2])
                if name == "v":
                    dst = v_sb[:, :, first - 2048:first - 2048 + C]
                elif name not in ("pu", "vm"):
                    earlier = [x for x in TR_CHUNKS if x < c and x % 2 == c % 2]
                    if earlier:
                        act.wait_ge(tr_psum, TR_DONE[earlier[-1], 1])
                act.wait_ge(rstd_done, CHUNKS[c][1] + 1)
                if name == "ki":
                    act.wait_ge(ki_psum, 1)
                for b in range(TB):
                    src = bank[3][:, b * w:(b + 1) * w] if name == "ki" else bank[2 * (c % 2) + b][:, 0:w]
                    ins = nc.scalar.activation(dst[:, b, 0:w], src, ACT.Copy,
                                               scale=rstd[:, CHUNKS[c][1], b:b + 1])
                ins.then_inc(z_evac, 1)

            def head_std(c):
                act.wait_ge(hvar_done, NORMED.index(c) + 1)
                nc.scalar.activation(hstat[:, 2, :], hstat[:, 1, :], ACT.Sqrt).then_inc(hstd_done, 1)

            def evac_transposed(t):
                _, c, part = TR_STEPS[t]
                name, _, first, _ = CHUNKS[c]
                act.wait_ge(tr_psum, t + 1)
                if name == "ki":
                    nc.scalar.activation(kiT, bank[4][:, 0:S], ACT.Copy).then_inc(tr_evac, 1)
                    return
                dst = {"qi": qiT, "q": qT, "k": kT, "qm": qmT, "km": kmT}[name]
                at = (4 * (first // C % 2) if name in ("qi", "q", "k") else 0) + 2 * part
                nc.scalar.activation(dst[:, at:at + 2, :], bank[4][:, :].rearrange("p (h t) -> p h t", h=2), ACT.Copy)\
                    .then_inc(tr_evac, 1)

            def index_relu(g):
                act.wait_ge(idx_psum, g + 1)
                if g >= 1:
                    act.wait_ge(idx_added, g)
                for h in range(2):
                    ins = nc.scalar.activation(relu[:, h, :, :], bank[6 + h][:, :].rearrange("p (j s) -> p j s", j=2),
                                               ACT.Relu, scale=IDX_SCALE)
                ins.then_inc(idx_relu, 1)

            def exponentials(i):
                act.wait_ge(logit_masked, i + 1)
                for b in range(TB):
                    ins = nc.scalar.activation(prob[:, i % 2, b, :], prob[:, i % 2, b, :], ACT.Exp,
                                               bias=astat[:, i % 2, 0, b:b + 1], accum_out=astat[:, i % 2, 1, b:b + 1])
                ins.then_inc(prob_exp, 1)

            def evac_probT(i):
                act.wait_ge(probT_psum, i + 1)
                if i >= 2:
                    act.wait_ge(av_psum, i - 1)
                nc.scalar.activation(probT[:, i % 2, :, :], bank[7][:, :].rearrange("p (b s) -> p b s", b=TB),
                                     ACT.Copy).then_inc(probT_evac, 1)

            def evac_av(i):
                act.wait_ge(av_psum, i + 1)
                nc.scalar.activation(mixed_of(i), bank[5][:, 0:S], ACT.Copy).then_inc(av_evac, 1)

            act.wait_ge(const_in, 16)
            xt_high(0, 0, 0, range(0, 4))
            make_hi(0)
            xt_high(0, 0, 0, range(4, 8))
            for n in range(N_OUT + 1):
                make_hi(n + 1)
                if n - 1 in TR_AT:
                    evac_transposed(TR_AT[n - 1])
                if n < 2:
                    xt_high(0, 0, 0, range(4 * n + 8, 4 * n + 12))
                if N_X - 3 <= n <= N_X:
                    k = 4 * (n - N_X + 3)
                    xt_high(1, 1, 1, range(k, k + 4))
                if n in EVAC_AT:
                    evac_chunk(EVAC_AT[n])
                if n - 1 in IDX_AT:
                    index_relu(IDX_AT[n - 1])
                if n - 1 in LOGIT_AT:
                    exponentials(LOGIT_AT[n - 1])
                if n - 1 in PROBT_AT:
                    evac_probT(PROBT_AT[n - 1])
                if n - 1 in AV_AT:
                    evac_av(AV_AT[n - 1])
                if n in XT_HEADS_AT:
                    for i in XT_HEADS_AT[n]:
                        act.wait_ge(av_evac, XT_HEADS[i] + 1)
                        nc.scalar.activation(XT[:, tile_of(XT_HEADS[i]), 0, :], mixed_of(XT_HEADS[i]), ACT.Copy)\
                            .then_inc(xt_hi, 1)
                if n - 1 in [FIRST_OF[c + 1] for c in NORMED]:
                    head_std(FIRST_OF.index(n - 1) - 1)
                if n in SQUARE_AT:
                    r, b = SQUARE_AT[n]
                    for arrived in (mem_in, [x_in])[r]:
                        act.wait_ge(arrived, 16)
                    if r == 1:
                        act.wait_ge(rstd_done, 1)
                    ins = square((ms, resid)[r][:, b, :], xs[:, b, :], b, 0)
                    if b == TB - 1:
                        ins.then_inc(ssq_done, 1)
                        row_std(r)
            load_table(ACT.Sqrt, 2)
            make_hi(N_OUT + 2)
            for g in range(2):
                act.wait_ge(poold_psum, g + 1)
                nc.scalar.activation(pooldT[:, 2 * g:2 * g + 2, :], bank[6 + g][:, :].rearrange("p (g t) -> p g t", g=2),
                                     ACT.Copy).then_inc(poold_evac, 1)
            make_hi(N_OUT + 3)
            for g in range(4):
                act.wait_ge(poolw_psum, g // 2 + 1)
                nc.scalar.activation(XT[:, 12 + g, 0, :], bank[6 + g // 2][:, (g % 2) * S:(g % 2 + 1) * S],
                                     ACT.Copy, scale=pscale[:, g:g + 1]).then_inc(xt_hi, 1)
            for oc in range(4):
                for n in range(N_OUT + 4 * oc + 2 + 2 * (oc == 0), N_OUT + 4 * oc + 6):
                    make_hi(n)
                act.wait_ge(h_added, oc + 1)
                for b in range(TB):
                    ins = square(resid[:, b, oc * C:(oc + 1) * C], hs[:, b, oc * C:(oc + 1) * C], b, oc)
            ins.then_inc(ssq_done, 1)
            row_std(2)
            xt_high(2, 3, 2)
            for m in range(17):
                if m < 16:
                    make_hi(N_WQ + m + 2)
                if m >= 1:
                    act.wait_ge(key_psum, m)
                    nc.scalar.activation(keysc[:, (m - 1) % 2, :, :],
                                         bank[4 + (m - 1) % 2][:, 0:S].rearrange("p (b n) -> p b n", b=TB), ACT.Copy)\
                        .then_inc(key_evac, 1)

            def gelu(i, j0, q):
                act.wait_ge(comb_done, i * 2 + (16 + q * QTR + j0 + 1))
                nc.scalar.activation(acts[:, bass.ds(i * 2 + j0, 1), :], comb[:, (u_first(q) + j0) % 2, :].unsqueeze(1), ACT.Gelu)\
                    .then_inc(gelu_done, 1)

            def hand_on(g, t0, s):
                act.wait_ge(g_evac, g + (GROUPS + 1))
                nc.scalar.activation(gts[:, bass.ds(t0 * QTR, GT * QTR)], stage[s][:, 0, :, :].rearrange("p t j -> p (t j)"),
                                     ACT.Copy).then_inc(gts_copied, 1)
                act.dma_start(spill[:, :, bass.ds(t0 * QTR, GT * QTR)].rearrange("q p f -> p q f"),
                              stage[s][:, 1:, :, :].rearrange("p q t j -> p q (t j)")).then_inc(spilled[s], 16)

            for q in range(QUARTERS):
                n0 = u_first(q)
                if q == 0:
                    load_table(ACT.Gelu, 0)
                    for first, end in ((0, EXP_TILE), (EXP_TILE, ROUTE - 1)):
                        with act.Fori(0, (end - first) // 2) as i:
                            for s in range(2):
                                make_hi_loop(i, n0 + first + s + 2)
                                gelu(i, first + s, 0)
                        if end == EXP_TILE:
                            act.wait_ge(pick_shift, 1)
                            nc.scalar.activation(pick, pick, ACT.Exp).then_inc(pick_exp, 1)
                            load_table(ACT.Gelu, 1)
                    make_hi(n0 + ROUTE + 1)
                    gelu(0, ROUTE - 1, 0)
                    for x, dst in enumerate((i1T, i2T)):
                        act.wait_ge(slots_psum, x + 1)
                        nc.scalar.activation(dst, bank[4 + x][:, 0:S], ACT.Copy).then_inc(slots_evac, 1)
                    with act.Fori(0, (QTR - 1 - ROUTE) // 2) as i:
                        for s in range(2):
                            make_hi_loop(i, n0 + ROUTE + s + 2)
                            gelu(i, ROUTE + s, 0)
                else:
                    with act.Fori(0, QTR // 2 - 1) as i:
                        for s in range(2):
                            make_hi_loop(i, n0 + s + 2)
                            gelu(i, s, q)
                            if q == 1:
                                hand_on(i * 2 + s, i * (2 * GT) + s * GT, s)
                    make_hi(n0 + QTR)
                    gelu(0, QTR - 2, q)
                    if q == 1:
                        hand_on(GROUPS - 2, S - 2 * GT, 0)
                        make_hi(n0 + QTR + 1)
                        gelu(0, QTR - 1, q)
                        hand_on(GROUPS - 1, S - GT, 1)
                for s in range(2):
                    act.wait_ge(prod_done, q * QTR + s + 1)
                    nc.scalar.activation(ah[:, s, :], prod[:, s, :], ACT.Copy).then_inc(ah_done, 1)
                if q != 1:
                    make_hi(n0 + QTR + 1)
                    gelu(0, QTR - 1, q)
                n0 = v_first(q)
                with act.Fori(0, QTR // 2 - 1) as i:
                    for s in range(2):
                        make_hi_loop(i, n0 + s + 2)
                        act.wait_ge(prod_done, i * 2 + (q * QTR + s + 3))
                        nc.scalar.activation(ah[:, s, :], prod[:, s, :], ACT.Copy).then_inc(ah_done, 1)
                if q < QUARTERS - 1:
                    for s in range(2):
                        make_hi(n0 + QTR + s)

        @block.vector
        def _(dve):
            steps = [0]

            def step(ins):
                steps[0] += 1
                ins.then_inc(dve_step, 1)

            def steps_but(k):
                dve.wait_ge(dve_step, steps[0] - k)

            def link(ins):
                step(ins)
                steps_but(0)

            tt = nc.vector.tensor_tensor

            def lo_dve(n, slot, share):
                dve.wait_ge(hi_done, n + 1)
                if not (isinstance(n, int) and n < 2):
                    dve.wait_ge(pe_used, n - 1)
                tt(lo[:, slot, share:UNIT], raw[:, slot, share:UNIT], hi[:, slot, share:UNIT].bitcast(F32),
                   ALU.subtract).then_inc(lo_dve_done, 1)

            def row_rstd(r):
                dve.wait_ge(ssq_done, r + 1)
                sums = ssq[:, :, 0]
                if r == 2:
                    link(nc.vector.tensor_reduce(ssum, ssq, AX_X, ALU.add))
                    sums = ssum
                nc.vector.tensor_scalar(var, sums, 1.0 / D, EPS, ALU.mult, ALU.add).then_inc(var_done, 1)
                dve.wait_ge(std_done, r + 1)
                nc.vector.reciprocal(rstd[:, r, :], rstd[:, r, :]).then_inc(rstd_done, 1)
                dve.wait_ge(rstd_done, r + 1)

            def xt_low(xt_round, gain, tiles=range(KT)):
                for k in tiles:
                    dve.wait_ge(xt_hi, xt_before(xt_round) + (k | 1) + 1)
                    src = xt_bank(xt_round, k // 2)[:, (k % 2) * S:(k % 2 + 1) * S]
                    nc.vector.scalar_tensor_tensor(XT[:, k, 1, :], src, gains[:, gain, k:k + 1],
                                                   XT[:, k, 0, :].bitcast(F32), ALU.mult, ALU.subtract).then_inc(xt_lo, 1)

            def heads_a(c):
                z = zt[:, c % 2].rearrange("p b (h d) -> p (b h) d", d=P)
                t = tmpA.rearrange("p (h d) -> p h d", d=P)
                dve.wait_ge(z_evac, c + 1)
                link(tt(t, z, z, ALU.mult))
                link(nc.vector.tensor_reduce(hstat[:, 0, :], t, AX_X, ALU.add))
                nc.vector.tensor_scalar(hstat[:, 1, :], hstat[:, 0, :], 1.0 / P, EPS, ALU.mult, ALU.add)\
                    .then_inc(hvar_done, 1)

            def signal_ready(ins, c):
                ins.then_inc(z_ready, 1)
                dve.wait_ge(z_ready, TR_CHUNKS.index(c) + 1)

            def heads_b(c):
                name = CHUNKS[c][0]
                dve.wait_ge(z_evac, c + 1)
                z = zt[:, c % 2]
                if c in NORMED:
                    z3 = z.rearrange("p b (h d) -> p (b h) d", d=P)
                    dve.wait_ge(hstd_done, NORMED.index(c) + 1)
                    link(nc.vector.reciprocal(hstat[:, 2, :], hstat[:, 2, :]))
                    link(tt(z3, z3, hstat[:, 2, :].unsqueeze(2).to_broadcast([P, 8, P]), ALU.mult))
                    gain = hgain[:, ("q", "k", "qm", "km").index(name), :].unsqueeze(1).to_broadcast([P, 8, P])
                    ins = tt(z3, z3, gain, ALU.mult)
                    if name in ("qm", "km"):
                        signal_ready(ins, c)
                        return
                    link(ins)
                rope = ropeA if name in ("q", "k") else ropeI
                f = 64 if name in ("q", "k") else 32
                w = 64 if name == "ki" else C
                nh = w // f
                z4 = z[:, :, 0:w].rearrange("p b (h f) -> p b h f", f=f)
                tA = tmpA[:, 0:2 * w].rearrange("p (b h f) -> p b h f", b=TB, f=f)
                tB = tmpB[:, 0:2 * w].rearrange("p (b h f) -> p b h f", b=TB, f=f)
                tt(tA, z4, rope[:, 0, :, :].unsqueeze(2).to_broadcast([P, TB, nh, f]), ALU.mult)
                link(tt(tB, z4, rope[:, 1, :, :].unsqueeze(2).to_broadcast([P, TB, nh, f]), ALU.mult))
                a5 = tmpA[:, 0:2 * w].rearrange("p (b h g f) -> p b h g f", b=TB, g=2, f=f)
                b5 = tmpB[:, 0:2 * w].rearrange("p (b h g f) -> p b h g f", b=TB, g=2, f=f)
                if name != "ki":
                    z5 = z.rearrange("p b (h g f) -> p b h g f", g=2, f=f)
                    tt(z5[:, :, :, 0, :], a5[:, :, :, 0, :], b5[:, :, :, 1, :], ALU.subtract)
                    signal_ready(tt(z5[:, :, :, 1, :], a5[:, :, :, 1, :], b5[:, :, :, 0, :], ALU.add), c)
                    return
                for copy in range(2):
                    tt(kidup[:, :, 64 * copy:64 * copy + f], a5[:, :, 0, 0, :], b5[:, :, 0, 1, :], ALU.subtract)
                    tt(kidup[:, :, 64 * copy + f:64 * copy + 2 * f], a5[:, :, 0, 1, :], b5[:, :, 0, 0, :], ALU.add)
                signal_ready(nc.vector.tensor_scalar(wi, z[:, :, 64:80], IDX_HEADS ** -0.5, None, ALU.mult), c)

            def index_add(g):
                b = g // 4
                dve.wait_ge(idx_relu, g + 1)
                for j in range(2):
                    for h in range(2):
                        head = 2 * (2 * (g % 4) + j) + h
                        ins = nc.vector.scalar_tensor_tensor(score[:, b, :], relu[:, h, j, :], wi[:, b, head:head + 1],
                                                             score[:, b, :], ALU.mult, ALU.add)
                        if (j, h) != (1, 1):
                            link(ins)
                ins.then_inc(idx_added, 1)
                dve.wait_ge(idx_added, g + 1)

            def take_eight(b):
                link(nc.vector.max(top8, score[:, b, :]))
                link(nc.vector.match_replace(score[:, b, :], top8, score[:, b, :], TAKEN))

            def softmax_head(i):
                r = i % 2
                dve.wait_ge(logit_psum, i + 1)
                if i >= 2:
                    dve.wait_ge(probT_psum, i - 1)
                src = bank[6][:, :].rearrange("p (b s) -> p b s", b=TB)
                if i >= M_HEADS:
                    link(nc.vector.scalar_tensor_tensor(prob[:, r, :, :], src, ATT_SCALE, mbias, ALU.mult, ALU.add))
                else:
                    link(nc.vector.tensor_scalar(prob[:, r, :, :], src, ATT_SCALE, None, ALU.mult))
                link(nc.vector.tensor_reduce(astat[:, r, 2, :], prob[:, r, :, :], AX_X, ALU.max))
                nc.vector.tensor_scalar(astat[:, r, 0, :], astat[:, r, 2, :], -1.0, None, ALU.mult)\
                    .then_inc(logit_masked, 1)
                dve.wait_ge(prob_exp, i + 1)
                link(nc.vector.reciprocal(astat[:, r, 3, :], astat[:, r, 1, :]))
                for b in range(TB):
                    ins = nc.vector.tensor_scalar(prob[:, r, b, :], prob[:, r, b, :], astat[:, r, 3, b:b + 1],
                                                  None, ALU.mult)
                ins.then_inc(prob_ready, 1)

            dve.wait_ge(const_in, 16)
            xt_low(0, 0, range(0, 4))
            lo_dve(0, 0, pool_share(0))
            xt_low(0, 0, range(4, 8))
            for n in range(N_OUT + 1):
                lo_dve(n + 1, (n + 1) % 2, pool_share(n + 1))
                if n < 2:
                    xt_low(0, 0, range(4 * n + 8, 4 * n + 12))
                if N_X - 3 <= n <= N_X:
                    k = 4 * (n - N_X + 3)
                    xt_low(1, 1, range(k, k + 4))
                if n == N_KI + 1:
                    dve.wait_ge(pe_used, N_KI + 1)
                    nc.vector.tensor_reduce(ki_z, bank[2][0:80, :].rearrange("p (n t) -> p t n", n=2), AX_X, ALU.add)\
                        .then_inc(ki_summed, 1)
                if n in [FIRST_OF[c + 1] for c in NORMED]:
                    heads_a(FIRST_OF.index(n) - 1)
                if n - 1 in IDX_AT:
                    index_add(IDX_AT[n - 1])
                if n in TOP_AT:
                    for _ in range(2):
                        take_eight(TOP_AT[n])
                if n == max(TOP_AT) + 1:
                    for b in range(TB):
                        link(nc.vector.tensor_scalar(mbias[:, b, :], score[:, b, :], 0.5 * (TAKEN + NOT_ADMISSIBLE),
                                                     -1e30, ALU.is_gt, ALU.mult))
                if n - 1 in LOGIT_AT:
                    softmax_head(LOGIT_AT[n - 1])
                if n - 1 in [FIRST_OF[c + 1] for c in TR_CHUNKS]:
                    heads_b(FIRST_OF.index(n - 1) - 1)
                if n in XT_HEADS_AT:
                    for i in XT_HEADS_AT[n]:
                        dve.wait_ge(xt_hi, xt_before(2) + i + 1)
                        k = tile_of(XT_HEADS[i])
                        tt(XT[:, k, 1, :], mixed_of(XT_HEADS[i]), XT[:, k, 0, :].bitcast(F32), ALU.subtract)\
                            .then_inc(xt_lo, 1)
                if n in SQUARE_AT and SQUARE_AT[n][1] == TB - 1:
                    row_rstd(SQUARE_AT[n][0])
                if n == 3:
                    dve.wait_ge(mixc_in, 32)
            for n in (N_OUT + 2, N_OUT + 3):
                lo_dve(n, n % 2, pool_share(n))
            for g in range(4):
                dve.wait_ge(xt_hi, xt_before(2) + HEADS + (g | 1) + 1)
                nc.vector.scalar_tensor_tensor(XT[:, 12 + g, 1, :], bank[6 + g // 2][:, (g % 2) * S:(g % 2 + 1) * S],
                                               pscale[:, g:g + 1], XT[:, 12 + g, 0, :].bitcast(F32),
                                               ALU.mult, ALU.subtract).then_inc(xt_lo, 1)
            for oc in range(4):
                for n in range(N_OUT + 4 * oc + 2 + 2 * (oc == 0), N_OUT + 4 * oc + 6):
                    lo_dve(n, n % 2, pool_share(n))
                dve.wait_ge(pe_used, N_OUT + 4 * oc + 4)
                for b in range(TB):
                    r = resid[:, b, oc * C:(oc + 1) * C]
                    ins = tt(r, r, bank[2 * ((oc + 1) % 2) + b][:, :], ALU.add)
                ins.then_inc(h_added, 1)
            row_rstd(2)
            for oc in range(4):
                cols = slice(oc * C, (oc + 1) * C)
                for b in range(TB):
                    ins = nc.vector.tensor_scalar(hs[:, b, cols], resid[:, b, cols], rstd[:, 2, b:b + 1], None, ALU.mult)
                ins.then_inc(rows_scaled, 1)
            xt_low(3, 2)

            def best_eight(lists, half):
                cols, others = slice(8 * half, 8 * half + 8), len(lists) - 1
                for values, best, where in lists:
                    steps_but(others)
                    step(nc.vector.max(best[:, cols], values))
                for values, best, where in lists:
                    steps_but(others)
                    step(nc.vector.max_index(where[:, cols], best[:, cols], values))
                if half == 0:
                    for values, best, where in lists:
                        steps_but(others)
                        step(nc.vector.match_replace(values, best[:, cols], values, TAKEN))

            def add_halves(b):
                nc.vector.tensor_reduce(comb[:, b, :], bank[b][:, :].rearrange("p (n t) -> p t n", n=2), AX_X, ALU.add)\
                    .then_inc(comb_done, 1)

            def combine_query(m):
                if m >= 2:
                    dve.wait_ge(key_psum, m - 1)
                dve.wait_ge(pe_used, N_WQ + m + 1)
                add_halves((N_WQ + m) % 2)

            def combine_tile(j, q, b):
                if not (isinstance(j, int) and q == 0 and j < 2):
                    dve.wait_ge(gelu_done, j + (q * QTR - 1))
                dve.wait_ge(pe_used, j + (u_first(q) + 1))
                add_halves(b)

            def key_list(m, b):
                return keysc[:, m % 2, b, :], v16[:, b, m, :], ix16[:, b, m, :]

            def pair_list(b, h):
                step(tt(cand[:, b, :].rearrange("p (a c) -> p a c", a=16),
                        v16[:, b, 2 * h, :].unsqueeze(2).to_broadcast([P, 16, 16]),
                        v16[:, b, 2 * h + 1, :].unsqueeze(1).to_broadcast([P, 16, 16]), ALU.add))
                return cand[:, b, :], pick[:, b, h, :], ci[:, b, 16 * h:16 * h + 16]

            for m in range(17):
                n = N_WQ + m
                lists = []
                if m < 16:
                    combine_query(m)
                if m >= 1:
                    dve.wait_ge(key_evac, m)
                    lists = [key_list(m - 1, b) for b in range(TB)]
                if m in PAIR_AT:
                    lists.append(pair_list(PAIR_AT.index(m), 0))
                    steps_but(0)
                if m >= 1:
                    best_eight(lists, 0)
                if m < 16:
                    lo_dve(n + 2, n % 2, pool_share(n + 2))
                if m >= 1:
                    best_eight(lists, 1)
            steps_but(0)

            def positions():
                nc.vector.tensor_copy(ixf, ix16)
                pairs = ci.rearrange("p b (h k) -> p (b h) k", h=8)
                halves = cab.rearrange("p b (h w) k -> p (b h) w k", w=2)
                nc.vector.tensor_single_scalar(halves[:, :, 0, :], pairs, 4, ALU.logical_shift_right)
                link(nc.vector.tensor_single_scalar(halves[:, :, 1, :], pairs, 15, ALU.bitwise_and))
                link(nc.vector.tensor_copy(abf, cab))

            def entries(b, first, end):
                for a in range(first, end):
                    ins = nc.vector.scalar_tensor_tensor(
                        sel[:, a, :, :], abf[:, b, :, :], float(a),
                        ixf[:, b, :, a].unsqueeze(2).to_broadcast([P, 16, 16]), ALU.is_equal, ALU.mult)
                link(ins)

            def picked(b, which):
                nc.vector.tensor_reduce(isel[:, which, b, :].rearrange("p (h k) -> p h k", h=8),
                                        sel.rearrange("p a (h w) k -> p w h k a", w=2)[:, which], AX_X, ALU.add).then_inc(slots_picked, 1)
                dve.wait_ge(slots_picked, 2 * b + which + 1)

            def take_weights(g_abs, t0, s):
                dve.wait_ge(g_psum, g_abs + 1)
                nc.vector.tensor_reduce(gts[:, bass.ds(t0 * QTR, GT * QTR)].rearrange("p (t j) -> p t j", j=QTR),
                                        bank[2 + s][:, :].rearrange("p (t n j) -> p t j n", t=GT, n=2), AX_X, ALU.add)\
                    .then_inc(g_evac, 1)

            def take_wide(g, s, uses):
                if not (isinstance(g, int) and g < 2):
                    dve.wait_ge(gts_copied, g - 1)
                    dve.wait_ge(spilled[s], uses * 16)
                dve.wait_ge(g_psum, g + (GROUPS + 1))
                for i, x in enumerate(WIDE_BANKS):
                    ins = nc.vector.tensor_reduce(
                        stage[s][:, :, 2 * i:2 * i + 2, :].rearrange("p q t j -> p t q j"),
                        bank[x][:, 0:4 * WIDE].rearrange("p (t q n j) -> p t q j n", t=2, n=2, j=QTR), AX_X, ALU.add)
                ins.then_inc(g_evac, 1)

            def one_hots(t0, s, tiles=slice(0, QTR), after=None):
                w = tiles.stop - tiles.start
                if after is not None:
                    dve.wait_ge(oh2_done, after)
                tt(eq2_of(s, w), iota[:, tiles].unsqueeze(1).to_broadcast([P, GT, w]),
                   i2T[:, bass.ds(t0, GT)].unsqueeze(2).to_broadcast([P, GT, w]), ALU.is_equal).then_inc(oh2_eq, 1)
                tt(oh1[:, s, :, :], iota.unsqueeze(1).to_broadcast([P, GT, P]),
                   i1T[:, bass.ds(t0, GT)].unsqueeze(2).to_broadcast([P, GT, P]), ALU.is_equal).then_inc(oh1_done, 1)

            def one_hots_wide(g, t0, s):
                one_hots(t0, s, slice(QTR, P), g + GROUPS)

            for j in range(ROUTE):
                n = N_EXP + j
                combine_tile(j, 0, n % 2)
                if j < 7:
                    lists = [pair_list(b, j + 1) for b in range(TB)]
                    best_eight(lists, 0)
                lo_dve(n + 2, n % 2, pool_share(n + 2))
                if j < 7:
                    best_eight(lists, 1)
                    steps_but(0)
                if j == 7:
                    link(nc.vector.tensor_copy(gsum, pick[:, :, :, 0]))
                    tt(pick, pick, gsum.unsqueeze(3).to_broadcast([P, TB, 8, 16]), ALU.subtract).then_inc(pick_shift, 1)
                    positions()
                if j == 8:
                    entries(0, 0, 12)
                if j == 9:
                    entries(0, 12, 16)
                    picked(0, 0)
                if j == 10:
                    picked(0, 1)
                    entries(1, 0, 5)
                if j == 11:
                    entries(1, 5, 16)
                if j == 12:
                    picked(1, 0)
                    dve.wait_ge(pick_exp, 1)
                    link(nc.vector.tensor_reduce(gsum, pick, AX_X, ALU.add))
                    link(nc.vector.reciprocal(gsum, gsum))
                    link(tt(pick, pick, gsum.unsqueeze(3).to_broadcast([P, TB, 8, 16]), ALU.mult))
                if j == 13:
                    picked(1, 1)
            dve.wait_ge(slots_psum, 3)
            link(nc.vector.tensor_copy(gT[:, 0, :].bitcast(F32R), bank[6][:, 0:S]))
            tt(gT[:, 1, :], bank[6][:, 0:S], gT[:, 0, :], ALU.subtract).then_inc(gsplit_done, 1)
            dve.wait_ge(slots_evac, 2)
            for s in range(2):
                one_hots(s * GT, s)
            with dve.Fori(0, (QTR - 1 - ROUTE) // 2 - 1) as i:
                for s in range(2):
                    n = N_EXP + ROUTE + s
                    combine_tile(i * 2 + (ROUTE + s), 0, n % 2)
                    lo_dve(i * 2 + (n + 2), n % 2, pool_share(n + 2))
                    for r in range(2):
                        take_weights(i * 4 + (2 * s + r), i * (4 * GT) + (2 * s + r) * GT, r)
                        one_hots(i * (4 * GT) + (2 * s + r + 2) * GT, r)
            for s in range(2):
                n = N_EXP + QTR - 3 + s
                combine_tile(QTR - 3 + s, 0, n % 2)
                lo_dve(n + 2, n % 2, pool_share(n + 2))
                for r in range(2):
                    g = GROUPS - 4 + 2 * s + r
                    take_weights(g, g * GT, r)
                    if s == 0:
                        one_hots((g + 2) * GT, r)

            for q in range(QUARTERS):
                if q >= 1:
                    n0 = u_first(q)
                    for s in range(2):
                        combine_tile(s, q, (n0 + s) % 2)
                        if q == 1:
                            take_wide(s, s, 0)
                        lo_dve(n0 + s + 2, (n0 + s) % 2, pool_share(n0 + 2))
                        if q == 1:
                            one_hots_wide(s + 2, (s + 2) * GT, s)
                    with dve.Fori(1, QTR // 2 - 1) as i:
                        for s in range(2):
                            combine_tile(i * 2 + s, q, (n0 + s) % 2)
                            if q == 1:
                                take_wide(i * 2 + s, s, i)
                            lo_dve(i * 2 + (n0 + s + 2), (n0 + s) % 2, pool_share(n0 + 2))
                            if q == 1:
                                one_hots_wide(i * 2 + (s + 2), i * (2 * GT) + (s + 2) * GT, s)
                    combine_tile(QTR - 2, q, (n0 + QTR - 2) % 2)
                    if q == 1:
                        take_wide(GROUPS - 2, 0, GROUPS // 2 - 1)
                    lo_dve(n0 + QTR, (n0 + QTR) % 2, pool_share(n0 + 2))

                def last_tile():
                    n = u_first(q) + QTR - 1
                    combine_tile(QTR - 1, q, n % 2)
                    if q == 1:
                        take_wide(GROUPS - 1, 1, GROUPS // 2 - 1)
                    lo_dve(n + 2, n % 2, pool_share(n + 2))

                def weighted(j, s):
                    if not isinstance(j, int):
                        j = bass.ds(j, 1)
                        x, g = acts[:, j, :].rearrange("p o t -> p (o t)"), gts_tj[:, :, j].rearrange("p t o -> p (t o)")
                    else:
                        x, g = acts[:, j, :], gts_tj[:, :, j]
                    tt(prod[:, s, :], x, g, ALU.mult).then_inc(prod_done, 1)

                def weighted_low(count, s):
                    dve.wait_ge(ah_done, count)
                    tt(al[:, s, :], prod[:, s, :], ah[:, s, :].bitcast(F32), ALU.subtract).then_inc(al_done, 1)

                if q == 1:
                    last_tile()
                if q == 0:
                    dve.wait_ge(g_evac, GROUPS)
                elif q == 1:
                    dve.wait_ge(gts_copied, GROUPS)
                else:
                    dve.wait_ge(gts_in, (q - 1) * 16 * (S * QTR // W_PART))
                dve.wait_ge(gelu_done, q * QTR + 2)
                for s in range(2):
                    weighted(s, s)
                for s in range(2):
                    weighted_low(q * QTR + s + 1, s)
                n0 = v_first(q)
                if q != 1:
                    last_tile()
                if q == 0:
                    for s in range(2):
                        one_hots_wide(s, s * GT, s)
                dve.wait_ge(gelu_done, (q + 1) * QTR)
                with dve.Fori(0, QTR // 2 - 1) as i:
                    for s in range(2):
                        dve.wait_ge(al_done, i * 2 + (q * QTR + s + 1))
                        weighted(i * 2 + (s + 2), s)
                        lo_dve(i * 2 + (n0 + s + 2), (n0 + s) % 2, pool_share(n0 + 2))
                        weighted_low(i * 2 + (q * QTR + s + 3), s)
                n = n0 + QTR
                if q < QUARTERS - 1:
                    lo_dve(n, n % 2, pool_share(n))
                for i, x in enumerate(V_BANKS):
                    if i < 7:
                        dve.wait_ge(v_psum, 7 * q + i + 1)
                    else:
                        dve.wait_ge(pe_used, n0 + QTR)
                    r = resid[:, x // 4, (x % 4) * C:(x % 4 + 1) * C]
                    tt(r, r, bank[x][:, :], ALU.add).then_inc(v_added, 1)
                if q < QUARTERS - 1:
                    lo_dve(n + 1, (n + 1) % 2, pool_share(n + 1))

        @block.tensor
        def _(pe):
            def unit_there(n):
                pe.wait_ge(hi_done, n + 1)
                pe.wait_ge(lo_dve_done, n + 1)
                pe.wait_ge(lo_pool_done, n + 1)

            def transpose_rows(src, xt_round, pairs=range(KT // 2)):
                banks = 3 if xt_round == 1 else 4
                for g in pairs:
                    if xt_round == 0 and g % 2 == 0:
                        pe.wait_ge(mem_in[g // 2], 16)
                    if g >= banks:
                        pe.wait_ge(xt_lo, xt_before(xt_round) + 2 * (g - banks) + 2)
                    for k in (2 * g, 2 * g + 1):
                        for b in range(TB):
                            ins = nc.tensor.transpose(xt_bank(xt_round, g)[:, (k % 2) * S + b * P:(k % 2) * S + (b + 1) * P],
                                                      src[:, b, k * P:(k + 1) * P], ident)
                    ins.then_inc(xt_psum, 1)

            def project(n, banks, k0, nk, w, xt_round=None):
                slot = n % 2
                unit_there(n)
                for k in range(nk):
                    if xt_round is not None:
                        pe.wait_ge(xt_lo, xt_before(xt_round) + k0 + k + 1)
                    wh, wl = hi[:, slot, k * w:(k + 1) * w], lo[:, slot, k * w:(k + 1) * w]
                    for b in range(TB):
                        xh, xl = (XT[:, k0 + k, part, b * P:(b + 1) * P] for part in range(2))
                        first, last = k0 + k == 0, k0 + k == KT - 1
                        o = bank[banks + b][:, 0:w]
                        nc.tensor.matmul(o, xh, wh, start=first, stop=False)
                        nc.tensor.matmul(o, xh, wl, start=False, stop=False)
                        ins = nc.tensor.matmul(o, xl, wh, start=False, stop=last)
                ins.then_inc(pe_used, 1)

            def project_ki(slot):
                unit_there(N_KI)
                for k in range(KT):
                    wh, wl = hi[:, slot, 80 * k:80 * k + 80], lo[:, slot, 80 * k:80 * k + 80]
                    nc.tensor.matmul(bank[2][0:80, :], wh, XT[:, k, :, :].rearrange("p n t -> p (n t)"),
                                     start=(k == 0), stop=False, skip_group_check=True)
                    ins = nc.tensor.matmul(bank[2][0:80, 0:S], wl, XT[:, k, 0, :], start=False, stop=(k == KT - 1),
                                           skip_group_check=True)
                ins.then_inc(pe_used, 1)

            def transpose_ki():
                pe.wait_ge(ki_summed, 1)
                for b in range(TB):
                    ins = nc.tensor.transpose(bank[3][:, 80 * b:80 * b + 80], ki_z[:, b * P:(b + 1) * P], ident[0:80, 0:80])
                ins.then_inc(ki_psum, 1)

            def transpose_heads(t):
                _, c, part = TR_STEPS[t]
                pe.wait_ge(z_ready, TR_CHUNKS.index(c) + 1)
                if t >= 1:
                    pe.wait_ge(tr_evac, t)
                for b in range(TB):
                    if CHUNKS[c][0] == "ki":
                        ins = nc.tensor.transpose(bank[4][:, b * P:(b + 1) * P], kidup[:, b, :], ident)
                        continue
                    for x in range(2):
                        d = (2 * part + x) * P
                        ins = nc.tensor.transpose(bank[4][:, x * S + b * P:x * S + (b + 1) * P],
                                                  zt[:, c % 2, b, d:d + P], ident)
                ins.then_inc(tr_psum, 1)

            def index_scores(g):
                b, pairs = g // 4, (2 * (g % 4), 2 * (g % 4) + 1)
                if g >= 1:
                    pe.wait_ge(idx_relu, g)
                pe.wait_ge(tr_evac, TR_DONE[5, 1])
                for j, pair in enumerate(pairs):
                    for h in range(2):
                        rows = slice(64 * h, 64 * h + 64)
                        ins = nc.tensor.matmul(bank[6 + h][:, j * S:(j + 1) * S], qiT[rows, pair, b * P:(b + 1) * P],
                                               kiT[rows, :], start=True, stop=True)
                ins.then_inc(idx_psum, 1)

            def logits(i):
                if i >= 1:
                    pe.wait_ge(logit_masked, i)
                if i == 0:
                    pe.wait_ge(tr_evac, TR_DONE[2, 1])
                if i == M_HEADS:
                    pe.wait_ge(idx_relu, 8)
                if i >= M_HEADS:
                    pe.wait_ge(tr_evac, TR_DONE[7 if i < M_HEADS + 4 else 9, 1])
                ql = mixed_of(i)
                kl = kmT[:, i, :] if i < M_HEADS else kT[:, i - M_HEADS, :]
                for b in range(TB):
                    ins = nc.tensor.matmul(bank[6][:, b * S:(b + 1) * S], ql[:, b * P:(b + 1) * P], kl,
                                           start=True, stop=True)
                ins.then_inc(logit_psum, 1)

            def transpose_probs(i):
                pe.wait_ge(prob_ready, i + 1)
                if i >= 1:
                    pe.wait_ge(probT_evac, i)
                for k in range(TB):
                    for b in range(TB):
                        ins = nc.tensor.transpose(bank[7][:, k * S + b * P:k * S + (b + 1) * P],
                                                  prob[:, i % 2, b, k * P:(k + 1) * P], ident)
                ins.then_inc(probT_psum, 1)

            def times_v(i):
                pe.wait_ge(probT_evac, i + 1)
                if i >= 1:
                    pe.wait_ge(av_evac, i)
                h = i - M_HEADS
                pe.wait_ge(z_evac, 2 if i < M_HEADS else 11 if h < 4 else 12)
                for k in range(TB):
                    vv = vm_sb[:, k, i * P:(i + 1) * P] if h < 0 else v_sb[:, k, h * P:(h + 1) * P]
                    ins = nc.tensor.matmul(bank[5][:, 0:S], vv, probT[:, i % 2, k, :], start=(k == 0), stop=(k == TB - 1))
                ins.then_inc(av_psum, 1)

            pe.wait_ge(const_in, 16)
            transpose_rows(ms, 0, range(0, 4))
            for n in range(N_OUT):
                c = CHUNK_OF[n]
                if n == FIRST_OF[c] and c >= 2:
                    pe.wait_ge(z_evac, c - 1)
                u, nk = n - FIRST_OF[c], KT // UNITS_OF[c]
                if n == N_KI:
                    project_ki(n % 2)
                else:
                    project(n, 2 * (c % 2), u * nk, nk, C, 0 if c == 0 else 1 if c == 2 else None)
                if n == N_KI + 1:
                    transpose_ki()
                if n < 2:
                    transpose_rows(ms, 0, range(2 * n + 4, 2 * n + 6))
                if n == N_X - 4:
                    pe.wait_ge(x_in, 16)
                    pe.wait_ge(xt_lo, xt_before(1))
                if N_X - 4 <= n < N_X:
                    g = 2 * (n - N_X + 4)
                    transpose_rows(resid, 1, range(g, g + 2))
                if n in TR_AT:
                    transpose_heads(TR_AT[n])
                if n in IDX_AT:
                    index_scores(IDX_AT[n])
                if n in LOGIT_AT:
                    logits(LOGIT_AT[n])
                if n in PROBT_AT:
                    transpose_probs(PROBT_AT[n])
                if n in AV_AT:
                    times_v(AV_AT[n])
            def pool_difference():
                pe.wait_ge(poolm_in, 16)
                pe.wait_ge(z_evac, NC)
                pe.wait_ge(probT_evac, HEADS)
                for g in range(4):
                    for b in range(TB):
                        ins = nc.tensor.matmul(bank[6 + g // 2][:, (g % 2) * S:(g % 2 + 1) * S],
                                               pu_sb[:, b, g * P:(g + 1) * P], poolM[:, g, b, :],
                                               start=(b == 0), stop=(b == TB - 1))
                    if g % 2:
                        ins.then_inc(poold_psum, 1)

            def pool_product():
                pe.wait_ge(poold_evac, 2)
                for g in range(4):
                    ins = nc.tensor.matmul(bank[6 + g // 2][:, (g % 2) * S:(g % 2 + 1) * S], poolW[:, g, :],
                                           pooldT[:, g, :], start=True, stop=True)
                    if g % 2:
                        ins.then_inc(poolw_psum, 1)

            for oc in range(4):
                if oc >= 2:
                    pe.wait_ge(h_added, oc - 1)
                for u in range(4):
                    if oc == 0 and u < 3:
                        pe.wait_ge(xt_lo, xt_before(2) + (4, 12, 12)[u])
                    if oc == 0 and u == 3:
                        pe.wait_ge(xt_lo, xt_before(3))
                    project(N_OUT + 4 * oc + u, 2 * ((oc + 1) % 2), 4 * u, 4, C)
                    if oc == 0 and u == 0:
                        pool_difference()
                    if oc == 0 and u == 1:
                        pool_product()
            for oc in range(4):
                pe.wait_ge(rows_scaled, oc + 1)
                transpose_rows(hs, 3, range(2 * oc, 2 * oc + 2))

            def expert_products(slot, b, xt_round=None):
                for k in range(KT):
                    if xt_round is not None:
                        pe.wait_ge(xt_lo, xt_before(xt_round) + k + 1)
                    wh, wl = hi[:, slot, k * P:(k + 1) * P], lo[:, slot, k * P:(k + 1) * P]
                    nc.tensor.matmul(bank[b][:, :], wh, XT[:, k, :, :].rearrange("p n t -> p (n t)"),
                                     start=(k == 0), stop=False, skip_group_check=True)
                    ins = nc.tensor.matmul(bank[b][:, 0:S], wl, XT[:, k, 0, :], start=False, stop=(k == KT - 1),
                                           skip_group_check=True)
                ins.then_inc(pe_used, 1)

            for m in range(17):
                if m < 16:
                    n = N_WQ + m
                    unit_there(n)
                    if m >= 2:
                        pe.wait_ge(comb_done, m - 1)
                    else:
                        pe.wait_ge(h_added, 4)
                    expert_products(n % 2, n % 2, 3 if m == 0 else None)
                if m >= 1:
                    pe.wait_ge(comb_done, m)
                    if m >= 3:
                        pe.wait_ge(key_evac, m - 2)
                    for b in range(TB):
                        ins = nc.tensor.matmul(bank[4 + (m - 1) % 2][:, b * P:(b + 1) * P],
                                               comb[:, (N_WQ + m - 1) % 2, b * P:(b + 1) * P], keysT[:, (m - 1) % 2, :],
                                               start=True, stop=True)
                    ins.then_inc(key_psum, 1)

            def tile(j, q, n0):
                unit_there(j + u_first(q))
                pe.wait_ge(comb_done, j + (16 + q * QTR - 1))
                expert_products(n0 % 2, n0 % 2)

            def group(g_abs, s):
                pe.wait_ge(oh1_done, g_abs + 1)
                pe.wait_ge(oh2_done, g_abs + 1)
                if not (isinstance(g_abs, int) and g_abs < 2):
                    pe.wait_ge(g_evac, g_abs - 1)
                for t in range(GT):
                    ins = nc.tensor.matmul(bank[2 + s][:, 2 * t * QTR:2 * (t + 1) * QTR].rearrange("p (n j) -> p n j", n=2),
                                           oh1[:, s, t, :], oh2_of(s, QTR)[:, t, 0, :, :], start=True, stop=True)
                ins.then_inc(g_psum, 1)

            def wide_group(g, s):
                pe.wait_ge(oh1_done, g + (GROUPS + 1))
                pe.wait_ge(oh2_done, g + (GROUPS + 1))
                pe.wait_ge(g_evac, g + GROUPS)
                for t in range(GT):
                    ins = nc.tensor.matmul(bank[WIDE_BANKS[t // 2]][:, t % 2 * 2 * WIDE:(t % 2 + 1) * 2 * WIDE], oh1[:, s, t, :],
                                           oh2_of(0, WIDE)[:, t, :, :, :].rearrange("p q n j -> p (q n j)"), start=True, stop=True)
                ins.then_inc(g_psum, 1)

            def v_products(n, slot, s, first=False, last=False, quarter_begun=None):
                unit_there(n)
                for x in V_BANKS:
                    b, c = x // 4, x % 4
                    if quarter_begun is not None and x == 0:
                        pe.wait_ge(comb_done, 16 + (quarter_begun + 1) * QTR)
                    xh, xl = ah[:, s, b * P:(b + 1) * P], al[:, s, b * P:(b + 1) * P]
                    vh, vl = hi[:, slot, c * C:(c + 1) * C], lo[:, slot, c * C:(c + 1) * C]
                    o = bank[x][:, :]
                    nc.tensor.matmul(o, xh, vh, start=first, stop=False, skip_group_check=True)
                    nc.tensor.matmul(o, xh, vl, start=False, stop=False, skip_group_check=True)
                    ins = nc.tensor.matmul(o, xl, vh, start=False, stop=last, skip_group_check=True)
                    if last and x != V_BANKS[-1]:
                        ins.then_inc(v_psum, 1)
                ins.then_inc(pe_used, 1)

            for q in range(QUARTERS):
                n0 = u_first(q)
                if q == 0:
                    with pe.Fori(0, ROUTE // 2) as i:
                        for s in range(2):
                            tile(i * 2 + s, 0, n0 + s)
                    tile(ROUTE - 1, 0, n0 + ROUTE - 1)
                    pe.wait_ge(slots_picked, 4)
                    pe.wait_ge(key_evac, 16)
                    for x in range(3):
                        for b in range(TB):
                            src = isel[:, x, b, :] if x < 2 else pick[:, b, :, :].rearrange("p h k -> p (h k)")
                            ins = nc.tensor.transpose(bank[4 + x][:, b * P:(b + 1) * P], src, ident)
                        ins.then_inc(slots_psum, 1)
                    for s in range(2):
                        tile(ROUTE + s, 0, n0 + ROUTE + s)
                        for r in range(2):
                            group(2 * s + r, r)
                    with pe.Fori(1, (QTR - 1 - ROUTE) // 2) as i:
                        for s in range(2):
                            tile(i * 2 + (ROUTE + s), 0, n0 + ROUTE + s)
                            for r in range(2):
                                group(i * 4 + (2 * s + r), r)
                else:
                    pe.wait_ge(v_added, 8 * (q - 1) + 1)
                    tile(0, q, n0)
                    if q == 1:
                        pe.wait_ge(v_added, 8 * (q - 1) + 6)
                        wide_group(0, 0)
                    pe.wait_ge(v_added, 8 * (q - 1) + 4)
                    tile(1, q, n0 + 1)
                    if q == 1:
                        wide_group(1, 1)
                    with pe.Fori(1, QTR // 2 - 1) as i:
                        for s in range(2):
                            tile(i * 2 + s, q, n0 + s)
                            if q == 1:
                                wide_group(i * 2 + s, s)
                    tile(QTR - 2, q, n0 + QTR - 2)
                    if q == 1:
                        wide_group(GROUPS - 2, 0)
                    pe.wait_ge(v_added, 8 * q)
                tile(QTR - 1, q, n0 + QTR - 1)
                if q == 1:
                    wide_group(GROUPS - 1, 1)
                pe.wait_ge(g_evac, min(q + 1, 2) * GROUPS)
                n0 = v_first(q)
                for s in range(2):
                    pe.wait_ge(al_done, q * QTR + s + 1)
                    v_products(n0 + s, (n0 + s) % 2, s, first=s == 0, quarter_begun=q if s == 0 else None)
                with pe.Fori(1, QTR // 2 - 1) as i:
                    for s in range(2):
                        pe.wait_ge(al_done, i * 2 + (q * QTR + s + 1))
                        v_products(i * 2 + (n0 + s), (n0 + s) % 2, s)
                for s in range(2):
                    pe.wait_ge(al_done, (q + 1) * QTR - 1 + s)
                    n = n0 + QTR - 2 + s
                    v_products(n, n % 2, s, last=s == 1)


def constants():
    pos = np.arange(S, dtype=np.float32)

    def rope(half):
        inv = (np.float32(10000.0) ** (-np.arange(half, dtype=np.float32) / np.float32(half))).astype(np.float32)
        ang = (pos[:, None] * inv[None, :]).astype(np.float32)
        t = np.stack([np.cos(ang), np.sin(ang)]).astype(np.float32)
        return np.ascontiguousarray(t.reshape(2, TB, P, half).transpose(2, 0, 1, 3))

    main = np.zeros((P, 256), np.float32)
    main[:, 0:128] = np.eye(P)
    main[:, 128:256] = np.arange(P)[None, :]
    chunk = np.arange(S) // 64
    adm = np.where(chunk[None, :] <= chunk[:, None], 0.0, NOT_ADMISSIBLE).astype(np.float32)
    adm = np.ascontiguousarray(adm.reshape(TB, P, S).transpose(1, 0, 2))
    pool = np.zeros((4, S, S), np.float32)
    for g, w in enumerate((2, 4, 8, 16)):
        for t in range(S):
            lo_ = max(t + 1 - w, 0)
            pool[g, lo_:t + 1, t] = np.float32(1.0) / np.float32(t + 1 - lo_)
            pool[g, t, t] -= 1.0
    pool = np.ascontiguousarray(pool.reshape(4, TB, P, S).transpose(2, 0, 1, 3))
    return main, adm, pool, rope(64).reshape(P, -1), rope(32).reshape(P, -1)


def units(w, width):
    n = w.shape[1] // width
    k = UNIT // width
    t = w.reshape(KT // k, k, P, n, width)
    return t.transpose(3, 0, 2, 1, 4).reshape(n * (KT // k), P, k * width)


def kernel(**inputs):
    import concourse.bacc as bacc
    from concourse.bass_utils import run_bass_kernel_spmd as run

    x = {k: np.asarray(v) for k, v in inputs.items()}
    w_in = x["w_in"][0]
    w_out = x["w_out"][0]
    w_out = np.concatenate([w_out[0:1024], w_out[1536:2048], w_out[1024:1536]])
    w_mix = np.concatenate([units((x["w_mem_kv"][0], w_in)[rows][:, f:f + w], C) for name, rows, f, w in CHUNKS
                            if name != "ki"] + [units(w_out, C), units(x["peer_w_q"][0], P)])
    _, _, f, w = CHUNKS[5]
    main, adm, pool, rope_a, rope_i = constants()
    arrays = {
        "x": x["x"][0], "mem": x["mem"][0], "w_mix": w_mix,
        "w_ki": w_in[:, f:f + w].reshape(KT, P, w).transpose(1, 0, 2).reshape(P, KT * w),
        "c_main": np.concatenate([main, x["peer_sub_keys_1"][0].T, x["peer_sub_keys_2"][0].T]
                                 + [x[g][0].reshape(KT, P).T for g in ("mem_norm_gain", "attn_norm_gain", "ffn_norm_gain")]
                                 + [x["pool_scale"][0].reshape(4, P).T], axis=1),
        "c_mix": np.concatenate([np.broadcast_to(x[g][0], (P, P)) for g in
                                 ("q_norm_gain", "k_norm_gain", "mq_norm_gain", "mk_norm_gain")]
                                + [rope_a, rope_i, x["pool_w"][0].transpose(1, 0, 2).reshape(P, 4 * P)], axis=1),
        "c_adm": adm, "c_pool": pool,
        "u": x["peer_u"][0].reshape(P, P, KT, P).transpose(1, 3, 2, 0).reshape(P, P, KT * P),
        "v": x["peer_v"][0].reshape(P, P, D),
    }
    arrays = {k: np.ascontiguousarray(v) for k, v in arrays.items()}
    nc = bacc.Bacc("TRN2", target_bir_lowering=False, num_devices=1)
    aps = {n: nc.dram_tensor(f"in_{n}", v.shape, F32, kind="ExternalInput").ap() for n, v in arrays.items()}
    out = nc.dram_tensor("out_h", (S, D), F32, kind="ExternalOutput").ap()
    build(nc, aps, out)
    r = run(nc, [{f"in_{n}": v for n, v in arrays.items()}], core_ids=[0])
    return r.results[0]["out_h"].reshape(1, S, D)
```
